# Optimizing a Trainium2 kernel written in Bass

```python
import math
import jax, jax.numpy as jnp
from jax import lax
import numpy as np

D_MODEL = 1024
BATCH = 1
SEQ = 256
DEPTH = 2

GRID_W = 64
CTX_LEN = 256
N_MIXERS = 3
D_FF = 4 * D_MODEL
DEEPNORM_ALPHA = (2 * DEPTH) ** 0.25
DEEPNORM_BETA = (8 * DEPTH) ** -0.25
LN_EPS = 1e-5
RMS_EPS = 1e-6

GLA_HEADS = 4
GLA_DK = D_MODEL // 2
GLA_DV = D_MODEL
GLA_HK = GLA_DK // GLA_HEADS
GLA_HV = GLA_DV // GLA_HEADS
GLA_RANK = 16
GLA_GATE_NORM = 16.0
GLA_CHUNK = 64
GLA_IN = 2 * GLA_DK + 2 * GLA_DV + 2 * GLA_RANK

SSD_DI = 2 * D_MODEL
SSD_HEADDIM = 64
SSD_HEADS = SSD_DI // SSD_HEADDIM
SSD_GROUPS = 8
SSD_REP = SSD_HEADS // SSD_GROUPS
SSD_STATE = 128
SSD_CONV = 5
SSD_CHUNK = 64
SSD_GN = SSD_GROUPS * SSD_STATE
SSD_CONV_DIM = SSD_DI + 2 * SSD_GN
SSD_IN = SSD_DI + SSD_CONV_DIM + 2 * SSD_HEADS

HY_ORDER = 2
HY_SHORT = 3
HY_EMB = 33
HY_FW = 64
HY_DECAY_TARGET = 1e-2
HY_FAST_DECAY = 0.3
HY_SLOW_DECAY = 1.5
HY_FILTER_GAIN = 0.05


def layer_norm(h, g, b):
    hf = h.astype(jnp.float32)
    mu = jnp.mean(hf, -1, keepdims=True)
    var = jnp.mean(jnp.square(hf - mu), -1, keepdims=True)
    return ((hf - mu) * lax.rsqrt(var + LN_EPS) * g + b).astype(h.dtype)

def rms_norm(h, g):
    hf = h.astype(jnp.float32)
    return (hf * lax.rsqrt(jnp.mean(hf * hf, -1, keepdims=True) + RMS_EPS) * g).astype(h.dtype)

def modulate(h, shift, scale):
    return h * (1 + scale) + shift

def snake(h):
    b, l, ch = h.shape
    rows = l // GRID_W
    g = h.reshape(b, rows, GRID_W, ch)
    odd = (jnp.arange(rows) % 2 == 1)[None, :, None, None]
    return jnp.where(odd, g[:, :, ::-1], g).reshape(b, l, ch)

def dwconv(u, w, bias):
    k, ch = w.shape
    out = lax.conv_general_dilated(u, w.astype(u.dtype)[:, None, :], window_strides=(1,),
                                   padding=[(k // 2, k // 2)],
                                   dimension_numbers=('NWC', 'WIO', 'NWC'),
                                   feature_group_count=ch)
    return out + bias

def to_heads(t, dh):
    b, l, _ = t.shape
    return t.reshape(b, l, -1, dh).transpose(0, 2, 1, 3)

def sq_relu_mlp(h, w1, w2):
    return jnp.square(jax.nn.relu(h @ w1)) @ w2

def gla_chunk_scan(q, k, v, log_a, s0):
    b, h, l, _ = q.shape
    nc = l // GLA_CHUNK

    def chunks(t):
        return jnp.moveaxis(t.reshape(b, h, nc, GLA_CHUNK, t.shape[-1]), 2, 0)

    mask = jnp.tril(jnp.ones((GLA_CHUNK, GLA_CHUNK), dtype=bool))[:, :, None]

    def step(s, inp):
        qi, ki, vi, gi = inp
        cum = jnp.cumsum(gi, axis=2)
        diff = cum[:, :, :, None, :] - cum[:, :, None, :, :]
        decay = jnp.exp(jnp.where(mask, diff, -jnp.inf))
        attn = jnp.einsum('bhid,bhjd,bhijd->bhij', qi, ki, decay)
        o = jnp.einsum('bhij,bhjv->bhiv', attn, vi) + jnp.einsum('bhid,bhdv->bhiv', qi * jnp.exp(cum), s)
        last = cum[:, :, -1:, :]
        s_new = s * jnp.exp(last[:, :, 0, :, None]) + jnp.einsum('bhjd,bhjv->bhdv', ki * jnp.exp(last - cum), vi)
        return s_new, o

    s_fin, oc = lax.scan(step, s0, tuple(map(chunks, (q, k, v, log_a))))
    return jnp.moveaxis(oc, 0, 2).reshape(b, h, l, v.shape[-1]), s_fin

def gla_mixer(uc, ul, w_in, w_a2, b_a2, norm_g, w_out, need_ctx):
    split_at = [GLA_DK, 2 * GLA_DK, 2 * GLA_DK + GLA_DV, 2 * GLA_DK + 2 * GLA_DV]

    def run(h, s_init, need_y):
        b, l, _ = h.shape
        q, k, v, g, a = jnp.split(h @ w_in, split_at, axis=-1)
        q = to_heads(q, GLA_HK) * GLA_HK ** -0.5
        k = to_heads(k, GLA_HK)
        v = to_heads(v, GLA_HV)
        logit = jnp.einsum('blzr,zrd->zbld', a.reshape(b, l, 2, GLA_RANK), w_a2) + b_a2[:, None, None, :]
        log_a = jax.nn.log_sigmoid(logit.astype(jnp.float32)) / GLA_GATE_NORM
        o_f, s_f = gla_chunk_scan(q, k, v, to_heads(log_a[0], GLA_HK), s_init[0])
        o_b, s_b = gla_chunk_scan(q[:, :, ::-1], k[:, :, ::-1], v[:, :, ::-1],
                                  to_heads(log_a[1], GLA_HK)[:, :, ::-1], s_init[1])
        if not need_y:
            return None, (s_f, s_b)
        o = rms_norm(o_f + o_b[:, :, ::-1], norm_g)
        o = o.transpose(0, 2, 1, 3).reshape(b, l, GLA_DV)
        return (o * jax.nn.silu(g)) @ w_out, (s_f, s_b)

    zeros = jnp.zeros((uc.shape[0], GLA_HEADS, GLA_HK, GLA_HV), jnp.float32)
    yc, ctx_states = run(uc, (zeros, zeros), need_ctx)
    yl, _ = run(ul, ctx_states, True)
    return yc, yl

def ssd_chunk_scan(xs, dt, a, bm, cm, s0):
    b, l = xs.shape[:2]
    nc = l // SSD_CHUNK

    def chunks(t):
        return jnp.moveaxis(t.reshape(b, nc, SSD_CHUNK, *t.shape[2:]), 1, 0)

    mask = jnp.tril(jnp.ones((SSD_CHUNK, SSD_CHUNK), dtype=bool))[None, :, :, None, None]

    def step(s, inp):
        xi, dti, bi, ci = inp
        cum = jnp.cumsum(dti * a, axis=1)
        seg = cum[:, :, None] - cum[:, None, :]
        decay = jnp.exp(jnp.where(mask, seg, -jnp.inf))
        xdt = xi * dti[..., None]
        cb = jnp.einsum('bign,bjgn->bijg', ci, bi)
        y = jnp.einsum('bijg,bijgr,bjgrp->bigrp', cb, decay, xdt)
        y = y + jnp.einsum('bign,bigr,bgrpn->bigrp', ci, jnp.exp(cum), s)
        last = cum[:, -1]
        s_new = s * jnp.exp(last)[..., None, None] + jnp.einsum(
            'bjgn,bjgr,bjgrp->bgrpn', bi, jnp.exp(last[:, None] - cum), xdt)
        return s_new, y

    s_fin, ys = lax.scan(step, s0, tuple(map(chunks, (xs, dt, bm, cm))))
    return jnp.moveaxis(ys, 0, 1).reshape(xs.shape), s_fin

def ssd_mixer(uc, ul, w_in, conv_w, conv_b, dt_bias, a_log, d_skip, norm_g, w_out, need_ctx):
    a = (-jnp.exp(a_log.astype(jnp.float32))).reshape(2, SSD_GROUPS, SSD_REP)
    d_gr = d_skip.reshape(SSD_GROUPS, SSD_REP, 1)

    def run(h, s_init, need_y):
        b, l, _ = h.shape
        z, xbc, dt = jnp.split(h @ w_in, [SSD_DI, SSD_DI + SSD_CONV_DIM], axis=-1)
        xbc = jax.nn.silu(dwconv(xbc, conv_w, conv_b))
        xs, bm, cm = jnp.split(xbc, [SSD_DI, SSD_DI + SSD_GN], axis=-1)
        xs = xs.reshape(b, l, SSD_GROUPS, SSD_REP, SSD_HEADDIM)
        bm = bm.reshape(b, l, SSD_GROUPS, SSD_STATE)
        cm = cm.reshape(b, l, SSD_GROUPS, SSD_STATE)
        dt = jax.nn.softplus(dt.astype(jnp.float32).reshape(b, l, 2, SSD_GROUPS, SSD_REP)
                             + dt_bias.reshape(2, SSD_GROUPS, SSD_REP))
        y_f, s_f = ssd_chunk_scan(xs, dt[:, :, 0], a[0], bm, cm, s_init[0])
        y_b, s_b = ssd_chunk_scan(xs[:, ::-1], dt[:, ::-1, 1], a[1], bm[:, ::-1], cm[:, ::-1], s_init[1])
        if not need_y:
            return None, (s_f, s_b)
        y = (y_f + y_b[:, ::-1] + xs * d_gr).reshape(b, l, SSD_DI)
        return rms_norm(y * jax.nn.silu(z), norm_g) @ w_out, (s_f, s_b)

    zeros = jnp.zeros((uc.shape[0], SSD_GROUPS, SSD_REP, SSD_HEADDIM, SSD_STATE), jnp.float32)
    yc, ctx_states = run(uc, (zeros, zeros), need_ctx)
    yl, _ = run(ul, ctx_states, True)
    return yc, yl

def hyena_pos_emb(l):
    bands = (HY_EMB - 1) // 2
    t = jnp.linspace(0.0, 1.0, l)[:, None]
    w = 2 * math.pi * jnp.arange(l, dtype=jnp.float32)[:, None] / l
    ang = jnp.linspace(1e-4, bands - 1, bands)[None, :] * w
    return jnp.concatenate([t, jnp.cos(ang), -jnp.sin(ang)], axis=-1)

def hyena_filters(l, f_w1, f_b1, f_w2, f_b2, f_w3, f_b3, f_w4, f_freq):
    act = lambda t: jnp.sin(f_freq * t)
    hh = act(hyena_pos_emb(l) @ f_w1 + f_b1)
    hh = act(hh @ f_w2 + f_b2)
    hh = act(hh @ f_w3 + f_b3)
    hh = (hh @ f_w4).reshape(l, HY_ORDER, 2, D_MODEL)
    t = jnp.linspace(0.0, 1.0, l)[:, None]
    deltas = jnp.abs(jnp.linspace(math.log(HY_DECAY_TARGET) / HY_FAST_DECAY,
                                  math.log(HY_DECAY_TARGET) / HY_SLOW_DECAY, D_MODEL))
    hh = hh * jnp.exp(-t * deltas)[:, None, None, :]
    fwd, bwd = hh[:, :, 0], hh[:, :, 1]
    return jnp.concatenate([fwd, jnp.zeros_like(fwd[:1]), bwd[:0:-1]], axis=0)

def fft_long_conv(u, h2l, bias):
    l = u.shape[1]
    uf = jnp.fft.rfft(u.astype(jnp.float32), n=2 * l, axis=1)
    hf = jnp.fft.rfft(h2l.astype(jnp.float32), n=2 * l, axis=0)
    y = jnp.fft.irfft(uf * hf, n=2 * l, axis=1)[:, :l]
    return (y + u * bias).astype(u.dtype)

def hyena_mixer(uc, ul, w_in, conv_w, conv_b, f_w1, f_b1, f_w2, f_b2, f_w3, f_b3, f_w4, f_freq,
                h_bias, w_out, need_ctx):
    def run(h):
        l = h.shape[1]
        v, x1, x2 = jnp.split(dwconv(h @ w_in, conv_w, conv_b), 3, axis=-1)
        filt = hyena_filters(l, f_w1, f_b1, f_w2, f_b2, f_w3, f_b3, f_w4, f_freq)
        z = x1 * fft_long_conv(v, filt[:, 0], h_bias[0])
        return (x2 * fft_long_conv(z, filt[:, 1], h_bias[1])) @ w_out

    yc = run(uc) if need_ctx else None
    return yc, run(ul)

def first_inputs(seed: int = 0) -> dict:
    key = jax.random.key(seed)
    ks = iter(jax.random.split(key, 40))
    nrm = lambda shape, s: jax.random.normal(next(ks), shape, jnp.float32) * s
    uni = lambda shape, lo, hi: jax.random.uniform(next(ks), shape, jnp.float32, minval=lo, maxval=hi)
    inv_softplus = lambda y: y + jnp.log(-jnp.expm1(-y))
    D = D_MODEL
    ng, ns, nh = (len(range(m, DEPTH, N_MIXERS)) for m in range(N_MIXERS))
    return {
        'x': nrm((BATCH, SEQ, D), 1.0),
        'c': nrm((BATCH, D), 1.0),
        'ctx': nrm((BATCH, CTX_LEN, D), 1.0),
        'c_ctx': nrm((D,), 1.0),
        'ada_w': nrm((DEPTH, D, 6 * D), D ** -0.5),
        'ada_b': nrm((DEPTH, 6 * D), 0.02),
        'ln_g': 1.0 + nrm((DEPTH, 2, D), 0.02),
        'ln_b': nrm((DEPTH, 2, D), 0.02),
        'ffn_w1': nrm((DEPTH, D, D_FF), D ** -0.5),
        'ffn_w2': nrm((DEPTH, D_FF, D), D_FF ** -0.5 * DEEPNORM_BETA),
        'gla_w_in': nrm((ng, D, GLA_IN), D ** -0.5),
        'gla_w_a2': nrm((ng, 2, GLA_RANK, GLA_DK), GLA_RANK ** -0.5),
        'gla_b_a2': nrm((ng, 2, GLA_DK), 0.1),
        'gla_norm': 1.0 + nrm((ng, GLA_HV), 0.02),
        'gla_w_out': nrm((ng, GLA_DV, D), GLA_DV ** -0.5 * DEEPNORM_BETA),
        'ssd_w_in': nrm((ns, D, SSD_IN), D ** -0.5),
        'ssd_conv_w': nrm((ns, SSD_CONV, SSD_CONV_DIM), SSD_CONV ** -0.5),
        'ssd_conv_b': nrm((ns, SSD_CONV_DIM), 0.02),
        'ssd_dt_bias': inv_softplus(jnp.exp(uni((ns, 2, SSD_HEADS), math.log(1e-3), math.log(1e-1)))),
        'ssd_a_log': jnp.log(uni((ns, 2, SSD_HEADS), 1.0, 16.0)),
        'ssd_d': 1.0 + nrm((ns, SSD_HEADS), 0.1),
        'ssd_norm': 1.0 + nrm((ns, SSD_DI), 0.02),
        'ssd_w_out': nrm((ns, SSD_DI, D), SSD_DI ** -0.5 * DEEPNORM_BETA),
        'hy_w_in': nrm((nh, D, 3 * D), D ** -0.5),
        'hy_conv_w': nrm((nh, HY_SHORT, 3 * D), HY_SHORT ** -0.5),
        'hy_conv_b': nrm((nh, 3 * D), 0.02),
        'hy_f_w1': nrm((nh, HY_EMB, HY_FW), HY_EMB ** -0.5),
        'hy_f_b1': nrm((nh, HY_FW), 0.1),
        'hy_f_w2': nrm((nh, HY_FW, HY_FW), HY_FW ** -0.5),
        'hy_f_b2': nrm((nh, HY_FW), 0.1),
        'hy_f_w3': nrm((nh, HY_FW, HY_FW), HY_FW ** -0.5),
        'hy_f_b3': nrm((nh, HY_FW), 0.1),
        'hy_f_w4': nrm((nh, HY_FW, HY_ORDER * 2 * D), HY_FW ** -0.5 * HY_FILTER_GAIN),
        'hy_f_freq': 1.0 + nrm((nh, HY_FW), 0.1),
        'hy_bias': nrm((nh, HY_ORDER, D), 1.0),
        'hy_w_out': nrm((nh, D, D), D ** -0.5 * DEEPNORM_BETA),
    }

def first_block(x, c, ctx, c_ctx, ada_w, ada_b, ln_g, ln_b, ffn_w1, ffn_w2,
              gla_w_in, gla_w_a2, gla_b_a2, gla_norm, gla_w_out,
              ssd_w_in, ssd_conv_w, ssd_conv_b, ssd_dt_bias, ssd_a_log, ssd_d, ssd_norm, ssd_w_out,
              hy_w_in, hy_conv_w, hy_conv_b, hy_f_w1, hy_f_b1, hy_f_w2, hy_f_b2, hy_f_w3, hy_f_b3,
              hy_f_w4, hy_f_freq, hy_bias, hy_w_out):
    hl, hc = x, ctx
    s_lat = jax.nn.silu(c)
    s_ctx = jax.nn.silu(c_ctx)
    for i in range(DEPTH):
        kind, j = i % N_MIXERS, i // N_MIXERS
        need_ctx = i < DEPTH - 1
        m_l = jnp.split((s_lat @ ada_w[i] + ada_b[i])[:, None, :], 6, axis=-1)
        m_c = jnp.split(s_ctx @ ada_w[i] + ada_b[i], 6, axis=-1)
        ul = snake(modulate(hl, m_l[0], m_l[1]))
        uc = modulate(hc, m_c[0], m_c[1])
        if kind == 0:
            yc, yl = gla_mixer(uc, ul, gla_w_in[j], gla_w_a2[j], gla_b_a2[j], gla_norm[j], gla_w_out[j], need_ctx)
        elif kind == 1:
            yc, yl = ssd_mixer(uc, ul, ssd_w_in[j], ssd_conv_w[j], ssd_conv_b[j], ssd_dt_bias[j],
                               ssd_a_log[j], ssd_d[j], ssd_norm[j], ssd_w_out[j], need_ctx)
        else:
            yc, yl = hyena_mixer(uc, ul, hy_w_in[j], hy_conv_w[j], hy_conv_b[j], hy_f_w1[j], hy_f_b1[j],
                                 hy_f_w2[j], hy_f_b2[j], hy_f_w3[j], hy_f_b3[j], hy_f_w4[j], hy_f_freq[j],
                                 hy_bias[j], hy_w_out[j], need_ctx)
        hl = layer_norm(DEEPNORM_ALPHA * hl + m_l[2] * snake(yl), ln_g[i, 0], ln_b[i, 0])
        hl = layer_norm(DEEPNORM_ALPHA * hl + m_l[5] * sq_relu_mlp(modulate(hl, m_l[3], m_l[4]), ffn_w1[i], ffn_w2[i]),
                        ln_g[i, 1], ln_b[i, 1])
        if need_ctx:
            hc = layer_norm(DEEPNORM_ALPHA * hc + m_c[2] * yc, ln_g[i, 0], ln_b[i, 0])
            hc = layer_norm(DEEPNORM_ALPHA * hc + m_c[5] * sq_relu_mlp(modulate(hc, m_c[3], m_c[4]), ffn_w1[i], ffn_w2[i]),
                            ln_g[i, 1], ln_b[i, 1])
    return hl


HEAD_DIM = 64
ROPE_BASE = 10000.0
EPS = 1e-6
NEG_INF = -1e30
Q_BLOCK = 128

NA_HEADS = 8
NA_WIN_R = 8
NA_WIN_C = 16
NA_QCB = 16
NA_KCB = 32
NA_WIDTH = NA_HEADS * HEAD_DIM
NA_SCALE = HEAD_DIM ** -0.5

MLA_HEADS = 8
MLA_Q_LORA = 384
MLA_KV_LORA = 256
MLA_NOPE = 64
MLA_ROPE = 32
MLA_V = 64
MLA_QK = MLA_NOPE + MLA_ROPE
MLA_WIDTH = MLA_HEADS * MLA_V
MLA_SCALE = MLA_QK ** -0.5

DIFF_HEADS = 4
DIFF_D = 64
DIFF_V = 2 * DIFF_D
DIFF_QK_WIDTH = DIFF_HEADS * 2 * DIFF_D
DIFF_WIDTH = DIFF_HEADS * DIFF_V
DIFF_SCALE = DIFF_D ** -0.5

N_BRANCH = 3
BRANCH_WIDTH = 512

IN_SPLITS = (NA_WIDTH, NA_WIDTH, NA_WIDTH,
             MLA_Q_LORA, MLA_KV_LORA, MLA_ROPE,
             DIFF_QK_WIDTH, DIFF_QK_WIDTH, DIFF_WIDTH,
             N_BRANCH * BRANCH_WIDTH, N_BRANCH * D_MODEL)
D_IN = sum(IN_SPLITS)


def rms_norm_2(x, g):
    xf = x.astype(jnp.float32)
    y = xf * lax.rsqrt(jnp.mean(xf * xf, axis=-1, keepdims=True) + EPS)
    return (y * g.astype(jnp.float32)).astype(x.dtype)

def axial_rope_tables(n_tokens, rot_dim):
    t = jnp.arange(n_tokens, dtype=jnp.int32)
    row = (t // GRID_W).astype(jnp.float32)
    col = (t % GRID_W).astype(jnp.float32)
    n_freq = rot_dim // 4
    inv = ROPE_BASE ** (-jnp.arange(n_freq, dtype=jnp.float32) / n_freq)
    ang = jnp.concatenate([row[:, None] * inv, col[:, None] * inv], axis=-1)
    return jnp.cos(ang), jnp.sin(ang)

def apply_rope(x, cos, sin):
    half = x.shape[-1] // 2
    shape = (cos.shape[0],) + (1,) * (x.ndim - 3) + (half,)
    cs = cos.reshape(shape).astype(x.dtype)
    sn = sin.reshape(shape).astype(x.dtype)
    x1, x2 = x[..., :half], x[..., half:]
    return jnp.concatenate([x1 * cs - x2 * sn, x2 * cs + x1 * sn], axis=-1)

def rope_tail(x, cos, sin, n_rot):
    return jnp.concatenate([x[..., :-n_rot], apply_rope(x[..., -n_rot:], cos, sin)], axis=-1)

def softmax_attend(q, k, v, scale):
    s = jnp.einsum('bqhd,bkhd->bhqk', q, k).astype(jnp.float32) * scale
    p = jax.nn.softmax(s, axis=-1).astype(v.dtype)
    return jnp.einsum('bhqk,bkhv->bqhv', p, v)

def diff_attend(q, k, v, lam, scale):
    s = jnp.einsum('bqhmd,bkhmd->bhmqk', q, k).astype(jnp.float32) * scale
    p = jax.nn.softmax(s, axis=-1)
    a = (p[:, :, 0] - lam * p[:, :, 1]).astype(v.dtype)
    return jnp.einsum('bhqk,bkhv->bqhv', a, v)

def blocked_queries(fn, q):
    B, T = q.shape[0], q.shape[1]
    nb = T // Q_BLOCK
    qb = jnp.moveaxis(q.reshape((B, nb, Q_BLOCK) + q.shape[2:]), 1, 0)
    out = lax.map(fn, qb)
    out = jnp.moveaxis(out, 0, 1)
    return out.reshape((B, T) + out.shape[3:])

def neighbourhood_attend(q, k, v, k_ctx, v_ctx, rpb):
    B, T, H, d = q.shape
    L = k_ctx.shape[1]
    rows = T // GRID_W
    kr = min(NA_WIN_R, rows)
    ncb = GRID_W // NA_QCB
    qcol = np.arange(GRID_W).reshape(ncb, NA_QCB)
    cstart = np.clip(qcol - NA_WIN_C // 2, 0, GRID_W - NA_WIN_C)
    band0 = np.clip(np.arange(ncb) * NA_QCB - NA_WIN_C // 2, 0, GRID_W - NA_KCB)
    kcol = band0[:, None] + np.arange(NA_KCB)
    kcol_f = np.tile(kcol, (1, kr))
    krow = np.repeat(np.arange(kr), NA_KCB)
    col_in = jnp.asarray((kcol_f[:, None, :] >= cstart[:, :, None])
                         & (kcol_f[:, None, :] < cstart[:, :, None] + NA_WIN_C))
    dc_idx = np.clip(kcol_f[:, None, :] - qcol[:, :, None], -(NA_WIN_C - 1), NA_WIN_C - 1) + (NA_WIN_C - 1)
    nk = kr * NA_KCB
    qg = q.reshape(B, rows, ncb, NA_QCB, H, d)
    kg = k.reshape(B, rows, GRID_W, H, d)
    vg = v.reshape(B, rows, GRID_W, H, d)

    def row_fn(r):
        rs = jnp.clip(r - kr // 2, 0, rows - kr)
        kb = lax.dynamic_slice_in_dim(kg, rs, kr, axis=1)[:, :, kcol]
        vb = lax.dynamic_slice_in_dim(vg, rs, kr, axis=1)[:, :, kcol]
        kb = kb.transpose(0, 2, 1, 3, 4, 5).reshape(B, ncb, nk, H, d)
        vb = vb.transpose(0, 2, 1, 3, 4, 5).reshape(B, ncb, nk, H, d)
        qr = lax.dynamic_index_in_dim(qg, r, axis=1, keepdims=False)
        dr = rs + krow - r + (NA_WIN_R - 1)
        bias = rpb[:, dr[None, None, :], dc_idx].astype(jnp.float32)
        s_lat = jnp.einsum('bnqhd,bnkhd->bhnqk', qr, kb).astype(jnp.float32) * NA_SCALE + bias
        s_lat = jnp.where(col_in, s_lat, NEG_INF)
        s_ctx = jnp.einsum('bnqhd,bkhd->bhnqk', qr, k_ctx).astype(jnp.float32) * NA_SCALE
        p = jax.nn.softmax(jnp.concatenate([s_ctx, s_lat], axis=-1), axis=-1).astype(v.dtype)
        return (jnp.einsum('bhnqk,bkhd->bnqhd', p[..., :L], v_ctx)
                + jnp.einsum('bhnqk,bnkhd->bnqhd', p[..., L:], vb))

    out = lax.map(row_fn, jnp.arange(rows))
    return out.transpose(1, 0, 2, 3, 4, 5).reshape(B, T, H * d)

def mixer_inputs(h, w_in_l, na_q_g, na_k_g, mla_cq_g, mla_ckv_g, w_uq_l, w_ukv_l,
                 mla_q_g, mla_k_g, diff_q_g, diff_k_g):
    lead = h.shape[:-1]
    split_points = [int(s) for s in np.cumsum(IN_SPLITS)[:-1]]
    (na_q, na_k, na_v, cq, ckv, k_rope, dq, dk, dv, z, gm) = jnp.split(h @ w_in_l, split_points, axis=-1)
    na_q = rms_norm_2(na_q.reshape(lead + (NA_HEADS, HEAD_DIM)), na_q_g)
    na_k = rms_norm_2(na_k.reshape(lead + (NA_HEADS, HEAD_DIM)), na_k_g)
    na_v = na_v.reshape(lead + (NA_HEADS, HEAD_DIM))
    mq = (rms_norm_2(cq, mla_cq_g) @ w_uq_l).reshape(lead + (MLA_HEADS, MLA_QK))
    kv = (rms_norm_2(ckv, mla_ckv_g) @ w_ukv_l).reshape(lead + (MLA_HEADS, MLA_NOPE + MLA_V))
    k_nope, mv = kv[..., :MLA_NOPE], kv[..., MLA_NOPE:]
    k_r = jnp.broadcast_to(k_rope[..., None, :], lead + (MLA_HEADS, MLA_ROPE))
    mk = rms_norm_2(jnp.concatenate([k_nope, k_r], axis=-1), mla_k_g)
    mq = rms_norm_2(mq, mla_q_g)
    dq = rms_norm_2(dq.reshape(lead + (DIFF_HEADS, 2, DIFF_D)), diff_q_g)
    dk = rms_norm_2(dk.reshape(lead + (DIFF_HEADS, 2, DIFF_D)), diff_k_g)
    dv = dv.reshape(lead + (DIFF_HEADS, DIFF_V))
    return (na_q, na_k, na_v, mq, mk, mv, dq, dk, dv, z, gm)

def diff_finish(o, subln_g, lam_init):
    o = rms_norm_2(o, subln_g) * (1.0 - lam_init)
    return o.reshape(o.shape[:-2] + (DIFF_WIDTH,))

def merge_branches(o_na, o_mla, o_diff, z, gm, w_br_l, w_out_l):
    z_na, z_mla, z_diff = jnp.split(z, N_BRANCH, axis=-1)
    g_na, g_mla, g_diff = jnp.split(gm, N_BRANCH, axis=-1)
    y = (jax.nn.sigmoid(g_na) * ((o_na * jax.nn.silu(z_na)) @ w_br_l[0])
         + jax.nn.sigmoid(g_mla) * ((o_mla * jax.nn.silu(z_mla)) @ w_br_l[1])
         + jax.nn.sigmoid(g_diff) * ((o_diff * jax.nn.silu(z_diff)) @ w_br_l[2]))
    return y @ w_out_l

def second_inputs(seed: int = 0) -> dict:
    key = jax.random.key(seed)
    ks = jax.random.split(key, 26)
    f32 = jnp.float32

    def nrm(k, shape, s):
        return jax.random.normal(k, shape, f32) * s

    def gain(k, shape):
        return 1.0 + 0.05 * jax.random.normal(k, shape, f32)

    D = D_MODEL
    return {
        'x': nrm(ks[0], (BATCH, SEQ, D), 1.0),
        'c': nrm(ks[1], (BATCH, D), 1.0),
        'ctx': nrm(ks[2], (BATCH, CTX_LEN, D), 1.0),
        'c_ctx': nrm(ks[3], (D,), 1.0),
        'norm_g': gain(ks[4], (DEPTH, D)),
        'w_ada': nrm(ks[5], (DEPTH, D, 3 * D), D ** -0.5),
        'b_ada': nrm(ks[6], (DEPTH, 3 * D), 0.02),
        'w_in': nrm(ks[7], (DEPTH, D, D_IN), D ** -0.5),
        'na_rpb': nrm(ks[8], (DEPTH, NA_HEADS, 2 * NA_WIN_R - 1, 2 * NA_WIN_C - 1), 0.1),
        'na_q_g': gain(ks[9], (DEPTH, HEAD_DIM)),
        'na_k_g': gain(ks[10], (DEPTH, HEAD_DIM)),
        'mla_cq_g': gain(ks[11], (DEPTH, MLA_Q_LORA)),
        'mla_ckv_g': gain(ks[12], (DEPTH, MLA_KV_LORA)),
        'w_uq': nrm(ks[13], (DEPTH, MLA_Q_LORA, MLA_HEADS * MLA_QK), MLA_Q_LORA ** -0.5),
        'w_ukv': nrm(ks[14], (DEPTH, MLA_KV_LORA, MLA_HEADS * (MLA_NOPE + MLA_V)), MLA_KV_LORA ** -0.5),
        'mla_q_g': gain(ks[15], (DEPTH, MLA_QK)),
        'mla_k_g': gain(ks[16], (DEPTH, MLA_QK)),
        'diff_q_g': gain(ks[17], (DEPTH, DIFF_D)),
        'diff_k_g': gain(ks[18], (DEPTH, DIFF_D)),
        'diff_lq1': nrm(ks[19], (DEPTH, DIFF_D), 0.1),
        'diff_lk1': nrm(ks[20], (DEPTH, DIFF_D), 0.1),
        'diff_lq2': nrm(ks[21], (DEPTH, DIFF_D), 0.1),
        'diff_lk2': nrm(ks[22], (DEPTH, DIFF_D), 0.1),
        'diff_subln_g': gain(ks[23], (DEPTH, DIFF_V)),
        'w_br': nrm(ks[24], (DEPTH, N_BRANCH, BRANCH_WIDTH, D), BRANCH_WIDTH ** -0.5),
        'w_out': nrm(ks[25], (DEPTH, D, D), D ** -0.5),
    }

def second_block(x, c, ctx, c_ctx, norm_g, w_ada, b_ada, w_in, na_rpb, na_q_g, na_k_g,
              mla_cq_g, mla_ckv_g, w_uq, w_ukv, mla_q_g, mla_k_g, diff_q_g, diff_k_g,
              diff_lq1, diff_lk1, diff_lq2, diff_lk2, diff_subln_g, w_br, w_out):
    B, T, _ = x.shape
    f32 = jnp.float32
    cos_m, sin_m = axial_rope_tables(T, MLA_ROPE)
    cos_d, sin_d = axial_rope_tables(T, DIFF_D)
    for l in range(DEPTH):
        last = l == DEPTH - 1
        lam_init = 0.8 - 0.6 * math.exp(-0.3 * l)
        lam = (jnp.exp(jnp.sum(diff_lq1[l].astype(f32) * diff_lk1[l].astype(f32)))
               - jnp.exp(jnp.sum(diff_lq2[l].astype(f32) * diff_lk2[l].astype(f32))) + lam_init)
        shift, scale, gate = jnp.split(jax.nn.silu(c) @ w_ada[l] + b_ada[l], 3, axis=-1)
        shift_c, scale_c, gate_c = jnp.split(jax.nn.silu(c_ctx) @ w_ada[l] + b_ada[l], 3, axis=-1)
        h = rms_norm_2(x, norm_g[l]) * (1.0 + scale[:, None]) + shift[:, None]
        hc = rms_norm_2(ctx, norm_g[l]) * (1.0 + scale_c) + shift_c
        params = (w_in[l], na_q_g[l], na_k_g[l], mla_cq_g[l], mla_ckv_g[l], w_uq[l], w_ukv[l],
                  mla_q_g[l], mla_k_g[l], diff_q_g[l], diff_k_g[l])
        (na_q, na_k, na_v, m_q, m_k, m_v, d_q, d_k, d_v, z, gm) = mixer_inputs(h, *params)
        (cna_q, cna_k, cna_v, cm_q, cm_k, cm_v, cd_q, cd_k, cd_v, cz, cgm) = mixer_inputs(hc, *params)
        m_q = rope_tail(m_q, cos_m, sin_m, MLA_ROPE)
        m_k = rope_tail(m_k, cos_m, sin_m, MLA_ROPE)
        d_q = apply_rope(d_q, cos_d, sin_d)
        d_k = apply_rope(d_k, cos_d, sin_d)
        m_k_all = jnp.concatenate([cm_k, m_k], axis=1)
        m_v_all = jnp.concatenate([cm_v, m_v], axis=1)
        d_k_all = jnp.concatenate([cd_k, d_k], axis=1)
        d_v_all = jnp.concatenate([cd_v, d_v], axis=1)
        o_na = neighbourhood_attend(na_q, na_k, na_v, cna_k, cna_v, na_rpb[l])
        o_mla = blocked_queries(lambda qb: softmax_attend(qb, m_k_all, m_v_all, MLA_SCALE), m_q)
        o_mla = o_mla.reshape(B, T, MLA_WIDTH)
        o_diff = blocked_queries(lambda qb: diff_attend(qb, d_k_all, d_v_all, lam, DIFF_SCALE), d_q)
        o_diff = diff_finish(o_diff, diff_subln_g[l], lam_init)
        x_new = x + gate[:, None] * merge_branches(o_na, o_mla, o_diff, z, gm, w_br[l], w_out[l])
        if not last:
            co_na = softmax_attend(cna_q, cna_k, cna_v, NA_SCALE).reshape(B, -1, NA_WIDTH)
            co_mla = softmax_attend(cm_q, cm_k, cm_v, MLA_SCALE).reshape(B, -1, MLA_WIDTH)
            co_diff = diff_finish(diff_attend(cd_q, cd_k, cd_v, lam, DIFF_SCALE), diff_subln_g[l], lam_init)
            ctx = ctx + gate_c * merge_branches(co_na, co_mla, co_diff, cz, cgm, w_br[l], w_out[l])
        x = x_new
    return x


def setup_inputs(seed=0):
    out = dict(first_inputs(seed))
    for name, value in second_inputs(seed + 1).items():
        if name != "x":
            out[name + "_2"] = value
    return out


def reference(
    x, c, ctx, c_ctx, ada_w, ada_b, ln_g, ln_b, ffn_w1, ffn_w2, gla_w_in, gla_w_a2, gla_b_a2,
    gla_norm, gla_w_out, ssd_w_in, ssd_conv_w, ssd_conv_b, ssd_dt_bias, ssd_a_log, ssd_d,
    ssd_norm, ssd_w_out, hy_w_in, hy_conv_w, hy_conv_b, hy_f_w1, hy_f_b1, hy_f_w2, hy_f_b2,
    hy_f_w3, hy_f_b3, hy_f_w4, hy_f_freq, hy_bias, hy_w_out, c_2, ctx_2, c_ctx_2, norm_g_2,
    w_ada_2, b_ada_2, w_in_2, na_rpb_2, na_q_g_2, na_k_g_2, mla_cq_g_2, mla_ckv_g_2, w_uq_2,
    w_ukv_2, mla_q_g_2, mla_k_g_2, diff_q_g_2, diff_k_g_2, diff_lq1_2, diff_lk1_2, diff_lq2_2,
    diff_lk2_2, diff_subln_g_2, w_br_2, w_out_2,
):
    x = first_block(
        x, c, ctx, c_ctx, ada_w, ada_b, ln_g, ln_b, ffn_w1, ffn_w2, gla_w_in, gla_w_a2,
        gla_b_a2, gla_norm, gla_w_out, ssd_w_in, ssd_conv_w, ssd_conv_b, ssd_dt_bias, ssd_a_log,
        ssd_d, ssd_norm, ssd_w_out, hy_w_in, hy_conv_w, hy_conv_b, hy_f_w1, hy_f_b1, hy_f_w2,
        hy_f_b2, hy_f_w3, hy_f_b3, hy_f_w4, hy_f_freq, hy_bias, hy_w_out,
    )
    return second_block(
        x, c_2, ctx_2, c_ctx_2, norm_g_2, w_ada_2, b_ada_2, w_in_2, na_rpb_2, na_q_g_2,
        na_k_g_2, mla_cq_g_2, mla_ckv_g_2, w_uq_2, w_ukv_2, mla_q_g_2, mla_k_g_2, diff_q_g_2,
        diff_k_g_2, diff_lq1_2, diff_lk1_2, diff_lq2_2, diff_lk2_2, diff_subln_g_2, w_br_2,
        w_out_2,
    )


_drawn_inputs = setup_inputs


def setup_inputs(seed=0):
    import zlib

    import numpy as np

    out = dict(_drawn_inputs(seed))
    spreads = {}
    factors = {'gla_b_a2': 5.122,
     'gla_norm': 8.0,
     'ssd_conv_b': 8.0,
     'ssd_d': 8.0,
     'ssd_norm': 8.0,
     'na_rpb_2': 8.0,
     'na_q_g_2': 8.0,
     'na_k_g_2': 8.0,
     'mla_cq_g_2': 8.0,
     'mla_ckv_g_2': 6.794,
     'mla_q_g_2': 8.0,
     'mla_k_g_2': 8.0,
     'diff_q_g_2': 8.0,
     'diff_k_g_2': 8.0,
     'diff_lk1_2': 5.045,
     'diff_lq2_2': 8.0,
     'diff_lk2_2': 3.063,
     'diff_subln_g_2': 3.768}
    for name, (base, spread) in spreads.items():
        noise = np.random.default_rng([zlib.crc32(name.encode()), seed]).standard_normal(out[name].shape)
        drawn = base * np.exp(spread * noise) if base else spread * noise
        out[name] = __import__('jax').numpy.asarray(drawn.astype(out[name].dtype))
    for name, factor in factors.items():
        out[name] = (out[name] * factor).astype(out[name].dtype)
    return out
```

```python
import math
from contextlib import ExitStack

import concourse.bass as bass
from concourse import mybir
from concourse.alu_op_type import AluOpType as ALU

F32 = mybir.dt.float32
F32R = mybir.dt.float32r
U8 = mybir.dt.uint8
ACT = mybir.ActivationFunctionType
AX_X = mybir.AxisListType.X

P = 128
D = 1024
KD = D // P
NCTX = 256
NLAT = 256
T = NCTX + NLAT
TT = T // P
CTX, LAT, ALL = (0, NCTX), (NCTX, T), (0, T)
ROW = 64
NCH = T // ROW
DEPTH = 2
ALPHA = (2 * DEPTH) ** 0.25
LN_EPS = 1e-5
RMS_EPS = 1e-6
DFF = 4 * D
GH, GDK, GDV = 4, 128, 256
GRANK = 16
GATE_NORM = 16.0
SG, SREP, SHD, SN = 8, 4, 64, 128
SH = SG * SREP
SDI = SH * SHD
SCONV = 5
XBC = SDI + 2 * SG * SN
LEVELS = [32, 16, 8, 4, 2, 1]
BW = 512
NAH, MLH, DFH = 8, 8, 4
MQK, MNOPE, MROPE = 96, 64, 32
QL, KVL = 384, 256
UQH = 3
NBANK = 4
RING = 3
SLOT = 1024
VK = SLOT // 512
VS = KD // VK
AHEAD = 2


def scan_order(z):
    half = NCH // 2
    return list(range(NCH)) if z == 0 else list(range(half - 1, -1, -1)) + list(range(NCH - 1, half - 1, -1))


class Build:

    def __init__(self, nc, dram, ctx):
        self.nc, self.dram, self.ctx = nc, dram, ctx
        self.sems = {}
        self.total = {}
        self.base = {}
        self.times = 1
        self.names = {}
        self.slots = []
        self.split_nth = []
        self.round_nth = []
        self.split_release = []
        self.partial = 0
        self.tiles = []
        self.release = []
        self.phases = {}
        self.counts = {"act": 0, "dve": 0}
        self.splits = {"act": 0, "dve": 0, "pool": 0}
        self.issued = 0
        self.next_split = {"act": 0, "dve": 0, "pool": 0}

    def sem(self, name):
        if name not in self.sems:
            self.sems[name] = self.ctx.enter_context(self.nc.semaphore(name))
            self.total[name] = self.base[name] = 0
        return self.sems[name]

    def tick(self, name, by=1):
        sem = self.sem(name)
        self.total[name] += by * self.times
        return sem

    def nth(self, name, n):
        self.sem(name)
        return self.base[name] + n

    def all(self, name):
        self.sem(name)
        return self.total[name]

    def stage(self):
        self.base = dict(self.total)
        return self.nc.Block(no_gpsimd_drain=True)

    def plan(self, phase, sources, ends, engine, low=None):
        first, t0 = len(self.slots), len(self.tiles)
        for n, (src, kt, w) in enumerate(sources):
            self.slots.append((src, kt, w, low))
            self.split_nth.append(self.splits[low] + 1 if low else None)
            self.round_nth.append(self.splits["act"] + 1 if low else None)
            if low:
                self.splits[low] += 1
                self.splits["act"] += 1
            for _ in range(ends[n]):
                self.tiles.append((first + n, engine, self.counts[engine]))
                self.counts[engine] += 1
            if ends[n]:
                self.release.append(("product_done", len(self.tiles)))
            else:
                self.partial += 1
                self.release.append(("weights_used", self.partial))
            if low:
                self.split_release.append(self.release[-1])
        self.phases[phase] = (first, len(sources), t0, len(self.tiles) - t0)

    def slot(self, n):
        _, kt, w, _ = self.slots[n]
        return self.wslots[:, n % RING, 0:kt * w].rearrange("p (k w) -> p k w", k=kt)

    def part(self, buffer, n):
        _, kt, w, _ = self.slots[n]
        return buffer[:, (self.round_nth[n] - 1) % RING, 0:kt * w].rearrange("p (k w) -> p k w", k=kt)

    def stream(self, sp, phase):
        first, count, _, _ = self.phases[phase]
        for n in range(self.issued, min(first + count + RING, len(self.slots))):
            src, kt, w, _ = self.slots[n]
            if n >= RING:
                sp.wait_ge(*self.slot_free(n - RING))
            sp.dma_start(self.slot(n), src.rearrange("(k p) w -> p k w", p=P))\
              .then_inc(self.tick(f"weights_in_{n % RING}", 16), 16)
            self.issued = n + 1

    def slot_free(self, n):
        if self.slots[n][3]:
            return self.weights_split(n)
        return self.sem(self.release[n][0]), self.release[n][1]

    def weights_in(self, n):
        return self.sem(f"weights_in_{n % RING}"), 16 * (n // RING + 1)

    def weights_split(self, n):
        return self.sem(f"weights_split_{self.slots[n][3]}"), self.split_nth[n]

    def round_weights(self, act, upto):
        upto = min(upto, len(self.slots) - 1)
        for n in range(self.next_split["act"], upto + 1):
            if self.slots[n][3]:
                if self.round_nth[n] > RING:
                    name, count = self.split_release[self.round_nth[n] - 1 - RING]
                    act.wait_ge(self.sem(name), count)
                act.wait_ge(*self.weights_in(n))
                act.activation(self.part(self.whi_r, n), self.slot(n), ACT.Copy)\
                    .then_inc(self.tick("weights_rounded"), 1)
        self.next_split["act"] = max(self.next_split["act"], upto + 1)

    def split_weights(self, engine, name, upto):
        upto = min(upto, len(self.slots) - 1)
        for n in range(self.next_split[name], upto + 1):
            if self.slots[n][3] == name:
                engine.wait_ge(self.sem("weights_rounded"), self.round_nth[n])
                engine.tensor_tensor(self.part(self.wlo_r, n), self.slot(n), self.part(self.whi, n), ALU.subtract)\
                    .then_inc(self.tick(f"weights_split_{name}"), 1)
        self.next_split[name] = max(self.next_split[name], upto + 1)

    def last_slot(self, g):
        return self.tiles[g][0]

    def passes(self, n, cols, parts):
        hi, lo = self.part(self.whi_r, n), self.part(self.wlo_r, n)
        out = []
        for k in range(self.slots[n][1]):
            xh, xl = parts(k)
            out += [(hi[:, k, cols], xh), (hi[:, k, cols], xl), (lo[:, k, cols], xh)]
        return out

    def passes_by_token(self, n, parts):
        hi, lo = self.part(self.whi_r, n), self.part(self.wlo_r, n)
        out = []
        for k in range(self.slots[n][1]):
            xh, xl = parts(k)
            out += [(xh, hi[:, k, :]), (xl, hi[:, k, :]), (xh, lo[:, k, :])]
        return out

    def input(self, cols):
        return lambda k: (self.UH_r[:, k, cols[0]:cols[1]], self.UL_r[:, k, cols[0]:cols[1]])

    def evacuated(self, g):
        _, engine, nth = self.tiles[g]
        return self.sem(f"evacuated_{engine}"), nth + 1

    def reads_out(self, g):
        return self.tick(f"evacuated_{self.tiles[g][1]}")

    def bank(self, g):
        return self.psum[:, g % NBANK, :]

    def product(self, pe, g, out_of, pairs, first=True, last=True, frees=True):
        if first and g >= NBANK:
            pe.wait_ge(*self.evacuated(g - NBANK))
        for i, (l, r) in enumerate(pairs):
            ins = pe.matmul(out_of(self.bank(g)), l, r, start=first and i == 0, stop=last and i == len(pairs) - 1,
                            skip_group_check=not (first and last))
        if last:
            ins.then_inc(self.tick("product_done"), 1)
        elif frees:
            ins.then_inc(self.tick("weights_used"), 1)

    def products(self, pe, phase, j, cols, parts):
        s0, _, t0, _ = self.phases[phase]
        pe.wait_ge(*self.weights_split(s0 + j))
        self.product(pe, t0 + j, lambda x: x[:, cols[0]:cols[1]], self.passes(s0 + j, slice(0, P), parts))

    def products_by_token(self, pe, phase, s, parts):
        s0, _, t0, _ = self.phases[phase]
        n, g0 = s0 + s, t0 + s // VS * TT
        pe.wait_ge(*self.weights_split(n))
        for j in range(TT):
            self.product(pe, g0 + j, lambda x: x,
                         self.passes_by_token(n, lambda k: parts(s % VS * VK + k, j)),
                         first=s % VS == 0, last=s % VS == VS - 1, frees=j == TT - 1)

    def tokens(self, k, j):
        return self.UH_r[:, k, j * P:(j + 1) * P], self.UL_r[:, k, j * P:(j + 1) * P]

    def sb(self, stack, name, shape, dt=F32):
        self.names[name] = self.names.get(name, -1) + 1
        if self.names[name]:
            name += f"_{self.names[name]}"
        return stack.enter_context(self.nc.sbuf_tensor(name, shape, dt))


def run_lengths(width, step):
    return [(a, min(a + step, width)) for a in range(0, width, step)]


def build(nc, d, out, dump=None, until=99):
    ctx = ExitStack()
    with ctx:
        b = Build(nc, d, ctx)
        b.psum = ctx.enter_context(nc.psum_tensor("psum", [P, 8, 512], F32))
        b.wslots = b.sb(ctx, "wslots", [P, RING, SLOT])
        b.whi = b.sb(ctx, "weights_hi", [P, RING, SLOT])
        b.wlo = b.sb(ctx, "weights_lo", [P, RING, SLOT])
        b.whi_r, b.wlo_r = b.whi[:].bitcast(F32R), b.wlo[:].bitcast(F32R)
        b.H1 = b.sb(ctx, "h1", [P, KD, T])
        b.H2 = b.sb(ctx, "h2", [P, KD, T])
        b.ident = b.sb(ctx, "ident", [P, P])
        b.snake = b.sb(ctx, "snake", [P, P])
        b.ones = b.sb(ctx, "ones", [P, P])
        b.half_ones = b.sb(ctx, "half_ones", [P, P])
        b.cols = b.sb(ctx, "cols", [P, 5, P])
        b.eps = b.sb(ctx, "eps", [P, 2])
        b.mod1 = b.sb(ctx, "mod1", [P, DEPTH, 48, 2])
        b.mod2 = b.sb(ctx, "mod2", [P, DEPTH, 24, 2])
        b.lam = b.sb(ctx, "lam", [P, DEPTH, 4])
        b.silu_c = b.sb(ctx, "silu_c", [P, 2, KD, 2])
        make_plan(b)
        load_stage(b)
        if until >= 1:
            adaln_stage(b)
        if until >= 2:
            gla_layer(b)
        if until >= 3:
            finish_layer(b, 0, ALL, b.H1)
        if until >= 4:
            ssd_layer(b)
        if until >= 5:
            finish_layer(b, 1, LAT, b.H2)
        if until >= 6:
            for l in range(DEPTH):
                attention_layer(b, l)
        store_stage(b, b.H2 if until >= 5 else b.H1, out, dump)


C_SILU, C_LNG, C_LNB, C_CONVB = (0, 0), (0, 32), (0, 64), (0, 96)
C_NORMG, C_SSDN, C_BADA2, C_GLAN, C_GLAB, C_CQG, C_CKVG, C_SUBLN = \
    (1, 0), (1, 16), (1, 32), (1, 80), (1, 82), (1, 90), (1, 96), (1, 100)
C_NAQ, C_NAK, C_DFQ, C_DFK, C_MLQ, C_MLK, C_LAM = (1, 102), (1, 104), (1, 106), (1, 108), (1, 110), (1, 112), (1, 114)
C_ADAB, C_DTB, C_ALOG = (2, 0), (2, 96), (2, 97)
C_CONVW = (3, 0)


def column(b, where, n, rows=P):
    t = where[0] + (where[1] + n) // P
    j = (where[1] + n) % P
    return b.cols[0:rows, t, j:j + 1]


def make_plan(b):
    d = b.dram

    def tiles(w, k):
        return [(w[:, a:e], k, e - a) for a, e in run_lengths(w.shape[1], P)]

    def wide(w):
        return [(w[k * P:(k + VK) * P, a:e], VK, e - a) for a, e in run_lengths(w.shape[1], 512)
                for k in range(0, w.shape[0] // P, VK)]

    def deep(w):
        return [(w[k * P:(k + KD) * P, a:e], KD, P) for a, e in run_lengths(w.shape[1], P)
                for k in range(0, w.shape[0] // P, KD)]

    def feature_major(phase, w, engine="act", low="pool"):
        s = tiles(w, KD)
        b.plan(phase, s, [1] * len(s), engine, low)

    def token_major(phase, w):
        s = wide(w)
        b.plan(phase, s, ([0] * (VS - 1) + [TT]) * (len(s) // VS), "act", "pool")

    def ada(phase, w):
        s = wide(w)
        b.plan(phase, s, ([0] * (VS - 1) + [1]) * (len(s) // VS), "act")

    for l in range(DEPTH):
        ada(f"ada1_{l}", d["ada_w"][l])
    for l in range(DEPTH):
        ada(f"ada2_{l}", d["w_ada_2"][l])
    g = d["gla_w_in"][0]
    feature_major("gla_a", g[:, 3104 - P:3104])
    feature_major("gla_qk", g[:, 0:1024])
    token_major("gla_v", g[:, 1024:2048])
    feature_major("gla_g", g[:, 2048:3072])
    feature_major("gla_out", d["gla_w_out"][0], "dve", "dve")

    def ffn(l):
        half = DFF // 2
        for i in range(2):
            feature_major(f"ffn{l}_up{i}", d["ffn_w1"][l][:, i * half:(i + 1) * half], "act", "dve")
            s = deep(d["ffn_w2"][l][i * half:(i + 1) * half, :])
            b.plan(f"ffn{l}_down{i}", s, [0, 1] * KD, "dve", "dve")

    ffn(0)
    s = d["ssd_w_in"][0]
    feature_major("ssd_dt", s[:, s.shape[1] - P:])
    feature_major("ssd_z", s[:, 0:SDI])
    feature_major("ssd_xbc", s[:, SDI:SDI + XBC], "dve")
    b.plan("ssd_out", deep(d["ssd_w_out"][0]), [0, 1] * KD, "dve", "dve")
    ffn(1)
    for l in range(DEPTH):
        w = d["w_in_2"][l]
        z0, g0 = 3744, 5280
        feature_major(f"na_qk{l}", w[:, 0:1024])
        token_major(f"na_v{l}", w[:, 1024:1536])
        feature_major(f"na_z{l}", w[:, z0:z0 + BW])
        feature_major(f"mla_cq{l}", w[:, 1536:1920])
        feature_major(f"mla_ckv{l}", w[:, 1920:2176])
        feature_major(f"mla_kr{l}", w[:, 2208 - P:2208])
        feature_major(f"mla_z{l}", w[:, z0 + BW:z0 + 2 * BW])
        u = d["w_uq_2"][l]
        b.plan(f"mla_uq{l}", [(u[:, a:e], QL // P, e - a) for a, e in run_lengths(MLH * MQK, UQH * MQK)],
               [UQH, UQH, MLH - 2 * UQH], "act")
        u = d["w_ukv_2"][l]
        b.plan(f"mla_ukv{l}", [(u[:, a:e], KVL // P, e - a) for a, e in run_lengths(MLH * P, 512)],
               [0, MLH + TT], "act")
        feature_major(f"diff_qk{l}", w[:, 2208:3232])
        token_major(f"diff_v{l}", w[:, 3232:3744])
        feature_major(f"diff_z{l}", w[:, z0 + 2 * BW:z0 + 3 * BW])
        for r in range(3):
            feature_major(f"gate{l}_{r}", w[:, g0 + r * D:g0 + (r + 1) * D], "act", "dve")
            u = d["w_br_2"][l, r]
            b.plan(f"branch{l}_{r}", [(u[:, a:e], BW // P, e - a) for a, e in run_lengths(D, 2 * P)], [2] * 4,
                   "dve", "dve")
        feature_major(f"merge{l}", d["w_out_2"][l], "dve", "dve")


def load_stage(b):
    d, nc = b.dram, b.nc
    st = ExitStack()
    with st:
        rows = b.sb(st, "rows", [P, 5, P])
        tok = b.sb(st, "tok", [P, 6, D])
        with b.stage() as block:
            @block.sync
            def _(sp):
                def ld(dst, src):
                    sp.dma_start(dst, src).then_inc(b.tick("vectors_in", 16), 16)

                for name, dst in (("c_ident", b.ident), ("c_snake", b.snake), ("c_ones", b.ones),
                                  ("c_half_ones", b.half_ones)):
                    sp.dma_start(dst[:], d[name]).then_inc(b.tick("constants_in", 16), 16)
                sp.wait_ge(b.sem("rows_cleared"), b.nth("rows_cleared", 1))
                for i, name in enumerate(("c", "c_ctx", "c_2", "c_ctx_2")):
                    v = d[name][0] if len(d[name].shape) == 2 else d[name]
                    ld(rows[8 * i:8 * i + 8, 0, :], v.rearrange("(k p) -> k p", p=P))
                ld(rows[32:64, 0, :], d["ln_g"].rearrange("l i (k p) -> (l i k) p", p=P))
                ld(rows[64:96, 0, :], d["ln_b"].rearrange("l i (k p) -> (l i k) p", p=P))
                ld(rows[96:128, 0, :], d["ssd_conv_b"][0].rearrange("(k p) -> k p", p=P))
                ld(rows[0:16, 1, :], d["norm_g_2"].rearrange("l (k p) -> (l k) p", p=P))
                ld(rows[16:32, 1, :], d["ssd_norm"][0].rearrange("(k p) -> k p", p=P))
                ld(rows[32:80, 1, :], d["b_ada_2"].rearrange("l (k p) -> (l k) p", p=P))
                ld(rows[80:82, 1, :], d["gla_norm"][0].rearrange("(k p) -> k p", p=P))
                ld(rows[82:90, 1, :], d["gla_b_a2"][0].rearrange("z (k p) -> (z k) p", p=P))
                ld(rows[90:96, 1, :], d["mla_cq_g_2"].rearrange("l (k p) -> (l k) p", p=P))
                ld(rows[96:100, 1, :], d["mla_ckv_g_2"].rearrange("l (k p) -> (l k) p", p=P))
                ld(rows[100:102, 1, :], d["diff_subln_g_2"])
                for i, name in enumerate(("na_q_g_2", "na_k_g_2", "diff_q_g_2", "diff_k_g_2")):
                    for h in range(2):
                        ld(rows[102 + 2 * i:104 + 2 * i, 1, 64 * h:64 * h + 64], d[name])
                ld(rows[110:112, 1, 0:MQK], d["mla_q_g_2"])
                ld(rows[112:114, 1, 0:MQK], d["mla_k_g_2"])
                for i, name in enumerate(("diff_lq1_2", "diff_lk1_2", "diff_lq2_2", "diff_lk2_2")):
                    ld(rows[114 + 2 * i:116 + 2 * i, 1, 0:64], d[name])
                ld(rows[0:96, 2, :], d["ada_b"].rearrange("l (k p) -> (l k) p", p=P))
                ld(rows[96:97, 2, 0:64], d["ssd_dt_bias"][0].rearrange("(a z) h -> a (z h)", a=1))
                ld(rows[97:98, 2, 0:64], d["ssd_a_log"][0].rearrange("(a z) h -> a (z h)", a=1))
                cw = d["ssd_conv_w"][0].rearrange("t (k p) -> (t k) p", p=P)
                ld(rows[:, 3, :], cw[0:P, :])
                ld(rows[0:32, 4, :], cw[P:160, :])
                for i, name in enumerate(("ctx", "x", "ctx_2")):
                    sp.dma_start(tok[:, 2 * i:2 * i + 2, :], d[name][0].rearrange("(t p) n -> p t n", p=P))\
                        .then_inc(b.tick("tokens_in", 16), 16)

            @block.gpsimd
            def _(pool):
                pool.memset(rows[:], 0.0).then_inc(b.tick("rows_cleared"), 1)
                pool.memset(b.eps[:, 0:1], LN_EPS / ALPHA ** 2)
                pool.memset(b.eps[:, 1:2], RMS_EPS)

            @block.tensor
            def _(pe):
                pe.wait_ge(b.sem("constants_in"), b.nth("constants_in", 64))
                pe.wait_ge(b.sem("vectors_in"), b.all("vectors_in"))
                for t in range(5):
                    ins = pe.transpose(b.psum[:, t // 4, t % 4 * P:(t % 4 + 1) * P], rows[:, t, :], b.ident[:])
                ins.then_inc(b.tick("columns_turned"), 1)
                pe.wait_ge(b.sem("tokens_in"), b.nth("tokens_in", 48))
                for i in range(3):
                    for k in range(KD):
                        n = i * KD + k
                        if n >= 4:
                            pe.wait_ge(b.sem("tile_copied"), b.nth("tile_copied", n - 3))
                        o = b.psum[:, 4 + n % 4, 0:2 * P]
                        for t in range(2):
                            ins = pe.matmul(o[:, t * P:(t + 1) * P], tok[:, 2 * i + t, k * P:(k + 1) * P],
                                            b.snake[:] if i == 1 else b.ident[:],
                                            start=t == 0, stop=t == 1, skip_group_check=True)
                        ins.then_inc(b.tick("tile_turned"), 1)

            @block.scalar
            def _(act):
                act.wait_ge(b.sem("columns_copied"), b.nth("columns_copied", 1))
                for blk in range(2):
                    for v in range(2):
                        act.activation(b.silu_c[:, blk, :, v], b.cols[:, 0, 16 * blk + 8 * v:16 * blk + 8 * v + 8],
                                       ACT.Silu)

            @block.vector
            def _(dve):
                dve.wait_ge(b.sem("columns_turned"), b.nth("columns_turned", 1))
                dve.tensor_copy(b.cols[:, 0:4, :], b.psum[:, 0, :].rearrange("p (a b) -> p a b", a=4))
                dve.tensor_copy(b.cols[:, 4, :], b.psum[:, 1, 0:P]).then_inc(b.tick("columns_copied"), 1)
                for i, dst in enumerate((b.H1[:, :, 0:NCTX], b.H1[:, :, NCTX:T], b.H2[:, :, 0:NCTX])):
                    for k in range(KD):
                        n = i * KD + k
                        dve.wait_ge(b.sem("tile_turned"), b.nth("tile_turned", n + 1))
                        dve.tensor_copy(dst[:, k, :], b.psum[:, 4 + n % 4, 0:2 * P])\
                            .then_inc(b.tick("tile_copied"), 1)


def adaln_stage(b):
    jobs = [(f"ada1_{l}", 0, l, 48) for l in range(DEPTH)] + [(f"ada2_{l}", 1, l, 24) for l in range(DEPTH)]
    st = ExitStack()
    with st:
        flat = b.sb(st, "ada_rows", [2, 2, 6 * D])
        with b.stage() as block:

            @block.sync
            def _(sp):
                for phase, *_ in jobs:
                    b.stream(sp, phase)

            @block.tensor
            def _(pe):
                def turn(j):
                    phase, blk, l, m = jobs[j]
                    first, _, t0, count = b.phases[phase]
                    pe.wait_ge(*b.evacuated(t0 + count - 1))
                    for i in range(m):
                        ins = pe.transpose(b.psum[:, 4 + j, 2 * i:2 * i + 2], flat[:, j % 2, i * P:(i + 1) * P],
                                           b.ident[0:2, 0:2])
                    ins.then_inc(b.tick("vectors_turned"), 1)

                for j, (phase, blk, l, m) in enumerate(jobs):
                    first, count, t0, _ = b.phases[phase]
                    for n in range(count):
                        pe.wait_ge(*b.weights_in(first + n))
                        w = b.slot(first + n)
                        b.product(pe, t0 + n // VS, lambda x: x[0:2, :],
                                  [(b.silu_c[:, blk, n % VS * VK + k, :], w[:, k, :]) for k in range(VK)],
                                  first=n % VS == 0, last=n % VS == VS - 1)
                        if n == 2 * VS - 1 and j >= 1:
                            turn(j - 1)
                turn(len(jobs) - 1)

            @block.scalar
            def _(act):
                for j, (phase, blk, l, m) in enumerate(jobs):
                    first, _, t0, count = b.phases[phase]
                    if j >= 2:
                        act.wait_ge(b.sem("vectors_turned"), b.nth("vectors_turned", j - 1))
                    for n in range(count):
                        b.round_weights(act, b.last_slot(t0 + n) + AHEAD)
                        act.wait_ge(b.sem("product_done"), t0 + n + 1)
                        ins = act.activation(flat[:, j % 2, n * 512:(n + 1) * 512], b.bank(t0 + n)[0:2, :], ACT.Copy)
                        ins.then_inc(b.reads_out(t0 + n), 1)

            @block.vector
            def _(dve):
                for j, (phase, blk, l, m) in enumerate(jobs):
                    dve.wait_ge(b.sem("vectors_turned"), b.nth("vectors_turned", j + 1))
                    mod = (b.mod1 if blk == 0 else b.mod2)[:, l]
                    where = C_ADAB if blk == 0 else C_BADA2
                    bias = b.cols[:, where[0], where[1] + l * m:where[1] + (l + 1) * m]
                    dve.tensor_tensor(
                        mod, b.psum[:, 4 + j, 0:2 * m].rearrange("p (m v) -> p m v", v=2),
                        bias.unsqueeze(2).broadcast_to([P, m, 2]), ALU.add).then_inc(b.tick("dve_step"), 1)
                    dve.wait_ge(b.sem("dve_step"), b.all("dve_step"))
                    scales = [1, 4] if blk == 0 else [1]
                    for s in scales:
                        v = mod[:, s * KD:(s + 1) * KD, :]
                        dve.tensor_scalar(v, v, 1.0, None, ALU.add).then_inc(b.tick("dve_step"), 1)
                    if blk == 0:
                        for s in (2, 5):
                            v = mod[:, s * KD:(s + 1) * KD, :]
                            dve.tensor_scalar(v, v, 1.0 / ALPHA, None, ALU.mult).then_inc(b.tick("dve_step"), 1)
                    else:
                        v = mod[:, KD:2 * KD, :]
                        dve.wait_ge(b.sem("dve_step"), b.all("dve_step"))
                        gain = b.cols[:, C_NORMG[0], C_NORMG[1] + l * KD:C_NORMG[1] + (l + 1) * KD]
                        dve.tensor_tensor(v, v, gain.unsqueeze(2).broadcast_to([P, KD, 2]), ALU.mult)\
                            .then_inc(b.tick("dve_step"), 1)


def input_parts(b, st, raw=None):
    b.UH = b.sb(st, "input_hi", [P, KD, T])
    b.UL = b.sb(st, "input_lo", [P, KD, T])
    b.UH_r, b.UL_r = b.UH[:].bitcast(F32R), b.UL[:].bitcast(F32R)
    if raw is not False:
        b.raw = b.sb(st, "input_raw", [P, 2, T]) if raw is None else raw


def raw_free(b, engine, k):
    if k >= 2:
        engine.wait_ge(b.sem("input_split"), b.nth("input_split", k - 1))


def modulate(b, dve, l, part, seg):
    sh, sc = (0, KD) if part == 0 else (3 * KD, 4 * KD)
    for k in range(KD):
        raw_free(b, dve, k)
        for v, (a, e) in enumerate((LAT, CTX)):
            if seg == LAT and v == 1:
                continue
            ins = dve.tensor_scalar(b.raw[:, k % 2, a:e], b.H1[:, k, a:e], b.mod1[:, l, sc + k, v:v + 1],
                                    b.mod1[:, l, sh + k, v:v + 1], ALU.mult, ALU.add)
        ins.then_inc(b.tick("modulated"), 1)
        if k:
            split_input(b, dve, k - 1, seg)
    split_input(b, dve, KD - 1, seg)


def round_input(b, act, k, seg):
    act.wait_ge(b.sem("modulated"), b.nth("modulated", k + 1))
    act.activation(b.UH_r[:, k, seg[0]:seg[1]], b.raw[:, k % 2, seg[0]:seg[1]], ACT.Copy)\
        .then_inc(b.tick("input_rounded"), 1)


def split_input(b, dve, k, seg):
    dve.wait_ge(b.sem("input_rounded"), b.nth("input_rounded", k + 1))
    dve.tensor_tensor(b.UL_r[:, k, seg[0]:seg[1]], b.raw[:, k % 2, seg[0]:seg[1]], b.UH[:, k, seg[0]:seg[1]],
                      ALU.subtract).then_inc(b.tick("input_split"), 1)


def residual(b, dve, l, gate, seg, g, m):
    b.split_weights(dve, "dve", b.last_slot(g) + AHEAD)
    dve.wait_ge(b.sem("product_done"), g + 1)
    for v, (a, e) in enumerate((LAT, CTX)):
        if seg == LAT and v == 1:
            continue
        ins = dve.scalar_tensor_tensor(b.H1[:, m, a:e], b.bank(g)[:, a:e], b.mod1[:, l, gate * KD + m, v:v + 1],
                                       b.H1[:, m, a:e], ALU.mult, ALU.add)
    ins.then_inc(b.reads_out(g), 1)


def layer_norm_stage(b, l, i, seg, dst):
    a, e = seg
    n = e - a
    st = ExitStack()
    with st:
        sq = b.sb(st, "ln_sq", [P, 2, n])
        mean = b.sb(st, "ln_mean", [P, n])
        rstd = b.sb(st, "ln_rstd", [P, n])
        with b.stage() as block:

            @block.tensor
            def _(pe):
                for k in range(KD):
                    ins = pe.matmul(b.psum[:, 4, 0:n], b.ones[:], b.H1[:, k, a:e], start=k == 0, stop=k == KD - 1)
                ins.then_inc(b.tick("sum_ready"), 1)
                for k in range(KD):
                    pe.wait_ge(b.sem("squared"), b.nth("squared", k + 1))
                    pe.matmul(b.psum[:, 5, 0:n], b.ones[:], sq[:, k % 2, :], start=k == 0, stop=k == KD - 1)\
                        .then_inc(b.tick("square_added"), 1)

            @block.scalar
            def _(act):
                for k in range(KD):
                    act.wait_ge(b.sem("centred"), b.nth("centred", k + 1))
                    if k >= 2:
                        act.wait_ge(b.sem("square_added"), b.nth("square_added", k - 1))
                    act.activation(sq[:, k % 2, :], b.H1[:, k, a:e], ACT.Square).then_inc(b.tick("squared"), 1)
                act.wait_ge(b.sem("square_added"), b.nth("square_added", KD))
                act.activation(rstd[:], b.psum[:, 5, 0:n], ACT.Sqrt, bias=b.eps[:, 0:1], scale=1.0 / D)\
                    .then_inc(b.tick("deviation_ready"), 1)
                for k in range(KD):
                    act.wait_ge(b.sem("scaled"), b.nth("scaled", k + 1))
                    where = (2 * l + i) * KD + k
                    act.activation(dst[:, k, a:e], b.H1[:, k, a:e], ACT.Identity,
                                   bias=column(b, C_LNB, where), scale=column(b, C_LNG, where))

            @block.vector
            def _(dve):
                dve.wait_ge(b.sem("sum_ready"), b.nth("sum_ready", 1))
                dve.tensor_scalar(mean[:], b.psum[:, 4, 0:n], 1.0 / D, None, ALU.mult).then_inc(b.tick("dve_step"), 1)
                dve.wait_ge(b.sem("dve_step"), b.all("dve_step"))
                for k in range(KD):
                    dve.tensor_tensor(b.H1[:, k, a:e], b.H1[:, k, a:e], mean[:], ALU.subtract)\
                        .then_inc(b.tick("centred"), 1)
                dve.wait_ge(b.sem("deviation_ready"), b.nth("deviation_ready", 1))
                dve.reciprocal(rstd[:], rstd[:]).then_inc(b.tick("dve_step"), 1)
                dve.wait_ge(b.sem("dve_step"), b.all("dve_step"))
                dve.wait_ge(b.sem("squared"), b.nth("squared", KD))
                for k in range(KD):
                    dve.wait_ge(b.sem("centred"), b.nth("centred", k + 1))
                    dve.tensor_tensor(b.H1[:, k, a:e], b.H1[:, k, a:e], rstd[:], ALU.mult).then_inc(b.tick("scaled"), 1)


def finish_layer(b, l, seg, dst):
    a, e = seg
    n = e - a
    HT = DFF // P // 2
    layer_norm_stage(b, l, 0, seg, b.H1)
    st = ExitStack()
    with st:
        input_parts(b, st)
        NH = 4
        hid = b.sb(st, "ffn_hidden", [P, NH, n])
        hid_hi = b.sb(st, "ffn_hidden_hi", [P, HT, n])
        hid_lo = b.sb(st, "ffn_hidden_lo", [P, HT, n])
        hid_lo_r, hid_hi_r = hid_lo[:].bitcast(F32R), hid_hi[:].bitcast(F32R)
        with b.stage() as block:
            ups = [b.phases[f"ffn{l}_up{i}"] for i in range(2)]
            downs = [b.phases[f"ffn{l}_down{i}"] for i in range(2)]

            @block.sync
            def _(sp):
                for i in range(2):
                    b.stream(sp, f"ffn{l}_up{i}")
                    b.stream(sp, f"ffn{l}_down{i}")

            @block.tensor
            def _(pe):
                pe.wait_ge(b.sem("input_split"), b.nth("input_split", KD))
                for i in range(2):
                    for j in range(HT):
                        b.products(pe, f"ffn{l}_up{i}", j, seg, b.input(seg))
                    s0, count, t0, _ = downs[i]
                    for s in range(count):
                        h0 = s % 2 * KD
                        pe.wait_ge(b.sem("hidden_split"), b.nth("hidden_split", i * HT + h0 + KD))
                        pe.wait_ge(*b.weights_split(s0 + s))
                        b.product(pe, t0 + s // 2, lambda x: x[:, a:e],
                                  b.passes(s0 + s, slice(0, P), lambda k: (hid_hi_r[:, h0 + k, :], hid_lo_r[:, h0 + k, :])),
                                  first=s % 2 == 0, last=s % 2 == 1)

            @block.scalar
            def _(act):
                def round_hidden(i, j):
                    act.wait_ge(b.sem("squared"), b.nth("squared", i * HT + j + 1))
                    act.activation(hid_hi_r[:, j, :], hid[:, j % NH, :], ACT.Copy).then_inc(b.tick("hidden_rounded"), 1)

                b.round_weights(act, ups[0][0])
                for k in range(KD):
                    round_input(b, act, k, seg)
                for i in range(2):
                    for j in range(HT):
                        g = ups[i][2] + j
                        b.round_weights(act, b.last_slot(g) + AHEAD)
                        act.wait_ge(b.sem("product_done"), g + 1)
                        if i * HT + j >= NH:
                            act.wait_ge(b.sem("hidden_split"), b.nth("hidden_split", i * HT + j - NH + 1))
                        act.activation(hid[:, j % NH, :], b.bank(g)[:, a:e], ACT.Relu).then_inc(b.reads_out(g), 1)
                        if j:
                            round_hidden(i, j - 1)
                    round_hidden(i, HT - 1)
                    b.round_weights(act, downs[i][0] + downs[i][1] - 1 + AHEAD)

            @block.vector
            def _(dve):
                def split_hidden(i, j):
                    dve.wait_ge(b.sem("hidden_rounded"), b.nth("hidden_rounded", i * HT + j + 1))
                    dve.tensor_tensor(hid_lo_r[:, j, :], hid[:, j % NH, :], hid_hi[:, j, :], ALU.subtract)\
                        .then_inc(b.tick("hidden_split"), 1)

                b.split_weights(dve, "dve", ups[0][0])
                modulate(b, dve, l, 1, seg)
                for i in range(2):
                    for j in range(HT):
                        g = ups[i][2] + j
                        b.split_weights(dve, "dve", b.last_slot(g) + AHEAD)
                        dve.wait_ge(*b.evacuated(g))
                        dve.tensor_tensor(hid[:, j % NH, :], hid[:, j % NH, :], hid[:, j % NH, :], ALU.mult)\
                            .then_inc(b.tick("squared"), 1)
                        if j:
                            split_hidden(i, j - 1)
                    split_hidden(i, HT - 1)
                    for m in range(KD):
                        residual(b, dve, l, 5, seg, downs[i][2] + m, m)
    layer_norm_stage(b, l, 1, seg, dst)


def gla_layer(b):
    st = ExitStack()
    with st:
        qk = b.sb(st, "gla_qk", [P, GH, 2, T])
        v = b.sb(st, "gla_v", [P, TT, D])
        gate = b.sb(st, "gla_gate", [P, KD, T])
        cum = b.sb(st, "gla_cum", [P, 2, GH, T])
        qT, kT = qk[:, :, 0, :], qk[:, :, 1, :]
        oT = qk[:].rearrange("p h a t -> p (h a) t")
        gla_project(b, qT, kT, v, gate, cum)
        gla_core(b, qT, kT, v, cum, oT)
        gla_out(b, oT, gate)


def gla_project(b, qT, kT, v, gate, cum):
    d = b.dram
    st = ExitStack()
    with st:
        input_parts(b, st)
        aT = b.sb(st, "gla_a", [2 * GRANK, T])
        wa = b.sb(st, "gla_wa", [2 * GRANK, 2, GH * GDK])
        reset = b.sb(st, "gla_reset", [P, T])
        lx = b.sb(st, "gla_lx", [P, 2, T])
        le = b.sb(st, "gla_le", [P, 2, T])
        with b.stage() as block:
            a0, _, at, _ = b.phases["gla_a"]
            q0, _, qt, _ = b.phases["gla_qk"]
            v0, _, vt, _ = b.phases["gla_v"]
            g0, _, gt, _ = b.phases["gla_g"]

            @block.sync
            def _(sp):
                sp.dma_start(reset[:], d["c_reset"]).then_inc(b.tick("gate_weights_in", 16), 16)
                sp.wait_ge(b.sem("padded"), b.nth("padded", 1))
                for z in range(2):
                    sp.dma_start(wa[z * GRANK:(z + 1) * GRANK, z, :], d["gla_w_a2"][0, z])\
                        .then_inc(b.tick("gate_weights_in", 16), 16)
                for phase in ("gla_a", "gla_qk", "gla_v", "gla_g"):
                    b.stream(sp, phase)

            @block.gpsimd
            def _(pool):
                pool.memset(wa[:], 0.0).then_inc(b.tick("padded"), 1)
                b.split_weights(pool, "pool", g0 + KD - 1)

            @block.tensor
            def _(pe):
                pe.wait_ge(b.sem("input_split"), b.nth("input_split", KD))
                b.products(pe, "gla_a", 0, ALL, b.input(ALL))

                def logits(n):
                    z, h = n // GH, n % GH
                    if n == 0:
                        pe.wait_ge(*b.evacuated(at))
                        pe.wait_ge(b.sem("gate_weights_in"), b.nth("gate_weights_in", 48))
                    if n >= 4:
                        pe.wait_ge(b.sem("logit_read"), b.nth("logit_read", n - 3))
                    pe.matmul(b.psum[:, 4 + n % 4, :], wa[:, z, h * GDK:(h + 1) * GDK], aT[:],
                                    start=True, stop=True).then_inc(b.tick("logit_ready"), 1)

                for j in range(KD):
                    b.products(pe, "gla_qk", j, ALL, b.input(ALL))
                    if j % 4 == 3:
                        for n in range(j - 3, j + 1):
                            logits(n)
                for s in range(2 * VS):
                    b.products_by_token(pe, "gla_v", s, b.tokens)
                for j in range(KD):
                    b.products(pe, "gla_g", j, ALL, b.input(ALL))

            @block.scalar
            def _(act):
                b.round_weights(act, a0)
                for k in range(KD):
                    round_input(b, act, k, ALL)
                b.round_weights(act, a0 + AHEAD)
                act.wait_ge(b.sem("product_done"), at + 1)
                act.activation(aT[:], b.bank(at)[P - 2 * GRANK:P, :], ACT.Copy).then_inc(b.reads_out(at), 1)

                def log_gate(n):
                    if n >= 2:
                        act.wait_ge(b.sem("gate_summed"), b.nth("gate_summed", n - 1))
                    act.wait_ge(b.sem("logit_ready"), b.nth("logit_ready", n + 1))
                    act.activation(lx[:, n % 2, :], b.psum[:, 4 + n % 4, :], ACT.Identity,
                                         bias=column(b, C_GLAB, n)).then_inc(b.tick("logit_read"), 1)
                    act.wait_ge(b.sem("logit_read"), b.nth("logit_read", n + 1))
                    for f, kw in ((ACT.Abs, {}), (ACT.Exp, {"scale": -1.0}), (ACT.Ln, {"bias": 1.0})):
                        src = lx if f == ACT.Abs else le
                        ins = act.activation(le[:, n % 2, :], src[:, n % 2, :], f, **kw)
                        if f == ACT.Ln:
                            ins.then_inc(b.tick("softplus_ready"), 1)
                        else:
                            ins.then_inc(b.tick("act_step"), 1)
                            act.wait_ge(b.sem("act_step"), b.all("act_step"))

                for s in range(2):
                    for j in range(4):
                        g = qt + 4 * s + j
                        b.round_weights(act, b.last_slot(g) + AHEAD)
                        act.wait_ge(b.sem("product_done"), g + 1)
                        dst = (qT, kT)[s][:, j, :]
                        act.activation(dst, b.bank(g), ACT.Copy, scale=GDK ** -0.5 if s == 0 else 1.0)\
                            .then_inc(b.reads_out(g), 1)
                    for n in range(4 * s, 4 * s + 4):
                        log_gate(n)
                for s in range(2):
                    for j in range(TT):
                        g = vt + TT * s + j
                        b.round_weights(act, b.last_slot(g) + AHEAD)
                        act.wait_ge(b.sem("product_done"), g + 1)
                        act.activation(v[:, j, s * 512:(s + 1) * 512], b.bank(g), ACT.Copy)\
                            .then_inc(b.reads_out(g), 1)
                for m in range(KD):
                    b.round_weights(act, b.last_slot(gt + m) + AHEAD)
                    act.wait_ge(b.sem("product_done"), gt + m + 1)
                    act.activation(gate[:, m, :], b.bank(gt + m), ACT.Silu).then_inc(b.reads_out(gt + m), 1)

            @block.vector
            def _(dve):
                modulate(b, dve, 0, 0, ALL)
                dve.wait_ge(b.sem("gate_weights_in"), b.nth("gate_weights_in", 48))
                for n in range(2 * GH):
                    z, h = n // GH, n % GH
                    dve.wait_ge(b.sem("softplus_ready"), b.nth("softplus_ready", n + 1))
                    dve.scalar_tensor_tensor(le[:, n % 2, :], lx[:, n % 2, :], 0.0, le[:, n % 2, :],
                                                       ALU.min, ALU.subtract).then_inc(b.tick("dve_step"), 1)
                    dve.wait_ge(b.sem("dve_step"), b.all("dve_step"))
                    if z == 0:
                        ins = dve.tensor_tensor_scan(cum[:, 0, h, :], reset[:], le[:, n % 2, :], 0.0,
                                                     ALU.mult, ALU.add)
                    else:
                        ins = dve.tensor_tensor_scan(cum[:, 1, h, ::-1], reset[:], le[:, n % 2, ::-1], 0.0,
                                                     ALU.mult, ALU.add)
                    ins.then_inc(b.tick("gate_summed"), 1)


def gla_core(b, qT, kT, v, cum, oT):
    d = b.dram
    INV = 1.0 / GATE_NORM
    NL = 2 * len(LEVELS)
    NI = NL + 1
    st = ExitStack()
    with st:
        masks = b.sb(st, "gla_masks", [P, NL, P], U8)
        diag2 = b.sb(st, "gla_diag2", [P, P])
        diff = b.sb(st, "gla_diff", [P, 2, T])
        ex = b.sb(st, "gla_ex", [P, 2, T])
        kq = b.sb(st, "gla_kq", [P, 2, T])
        score = b.sb(st, "gla_score", [P, 2, TT, P])
        hd = b.sb(st, "gla_hd", [P, 2, T])
        ek = b.sb(st, "gla_ek", [P, 2, T])
        eq = b.sb(st, "gla_eq", [P, 2, T])
        el = b.sb(st, "gla_el", [P, 2, NCH])
        khT = b.sb(st, "gla_khT", [P, 2, T])
        qhT = b.sb(st, "gla_qhT", [P, 2, T])
        kh = b.sb(st, "gla_kh", [P, 2, TT, P])
        state = b.sb(st, "gla_state", [P, 2, NCH - 1, GDV])

        wide_masks = state[:].rearrange("p z c v -> p (z c v)")[:, 0:NL * P]

        def level(n):
            return n // len(LEVELS), LEVELS[n % len(LEVELS)]

        def sides(x, z, s):
            y = x.rearrange("p (n i s) -> p n i s", i=2, s=s)
            return y[:, :, z, :], y[:, :, 1 - z, :]

        with b.stage() as block:

            @block.sync
            def _(sp):
                sp.dma_start(wide_masks, d["c_gla_masks"]).then_inc(b.tick("masks_in", 16), 16)
                sp.dma_start(diag2[:], d["c_diag2"]).then_inc(b.tick("masks_in", 16), 16)

            @block.tensor
            def _(pe):
                for h in range(GH):
                    for it in range(NI):
                        m, q = h * NI + it, h * NL + it - 1
                        if m >= 2:
                            pe.wait_ge(b.sem("score_taken"), b.nth("score_taken", m - 1))
                        if it:
                            pe.wait_ge(b.sem("key_side"), b.nth("key_side", q + 1))
                            pe.wait_ge(b.sem("query_side"), b.nth("query_side", q + 1))
                        for t in range(TT):
                            cols = slice(t * P, (t + 1) * P)
                            l, r = (kT[:, h, cols], qT[:, h, cols]) if it == 0 else (kq[:, q % 2, cols],) * 2
                            ins = pe.matmul(b.psum[:, 4 + m % 2, cols], l, r, start=t == 0, stop=t == TT - 1,
                                            skip_group_check=True)
                        ins.then_inc(b.tick("score_made"), 1)
                    for z in range(2):
                        u = 2 * h + z
                        pe.wait_ge(b.sem("key_hat"), b.nth("key_hat", u + 1))
                        if u >= 1:
                            pe.wait_ge(b.sem("key_hat_copied"), b.nth("key_hat_copied", u))
                        for t in range(TT):
                            ins = pe.transpose(b.psum[:, 6, t * P:(t + 1) * P], khT[:, z, t * P:(t + 1) * P], b.ident[:])
                        ins.then_inc(b.tick("key_hat_turned"), 1)
                    for z in range(2):
                        u = 2 * h + z
                        pe.wait_ge(b.sem("key_hat_copied"), b.nth("key_hat_copied", u + 1))
                        for i, c in enumerate(scan_order(z)[:-1]):
                            x = u * (NCH - 1) + i
                            if x >= 2:
                                pe.wait_ge(b.sem("state_ready"), b.nth("state_ready", x - 1))
                            rows = slice(ROW * (c % 2), ROW * (c % 2) + ROW)
                            pe.matmul(b.psum[:, 2 + x % 2, 0:GDV], kh[rows, z, c // 2, :],
                                            v[rows, c // 2, h * GDV:(h + 1) * GDV], start=True, stop=True,
                                            skip_group_check=True).then_inc(b.tick("state_addend"), 1)
                    pe.wait_ge(b.sem("score_taken"), b.nth("score_taken", (h + 1) * NI))
                    pe.wait_ge(b.sem("state_ready"), b.nth("state_ready", 2 * (h + 1) * (NCH - 1)))
                    pe.wait_ge(b.sem("query_hat"), b.nth("query_hat", 2 * (h + 1)))
                    if h:
                        pe.wait_ge(b.sem("output_copied"), b.nth("output_copied", 2 * h))
                    for vt in range(2):
                        o = b.psum[:, vt, :]
                        for t in range(TT):
                            pe.matmul(o[:, t * P:(t + 1) * P], v[:, t, h * GDV + vt * P:h * GDV + (vt + 1) * P],
                                      score[:, h % 2, t, :], start=t == 0, stop=False, skip_group_check=True)
                        for z in range(2):
                            for i, c in enumerate(scan_order(z)):
                                if i:
                                    ins = pe.matmul(o[:, c * ROW:(c + 1) * ROW],
                                                    state[:, z, i - 1, vt * P:(vt + 1) * P],
                                                    qhT[:, z, c * ROW:(c + 1) * ROW], start=False,
                                                    stop=z == 1 and i == NCH - 1, skip_group_check=True)
                        ins.then_inc(b.tick("output_made"), 1)

            @block.scalar
            def _(act):
                def copy_output(h):
                    for vt in range(2):
                        act.wait_ge(b.sem("output_made"), b.nth("output_made", 2 * h + vt + 1))
                        act.activation(oT[:, 2 * h + vt, :], b.psum[:, vt, :], ACT.Copy)\
                            .then_inc(b.tick("output_copied"), 1)

                for h in range(GH):
                    for n in range(NL):
                        q = h * NL + n
                        z, s = level(n)
                        act.wait_ge(b.sem("diff_ready"), b.nth("diff_ready", q + 1))
                        if q >= 2:
                            act.wait_ge(b.sem("key_side"), b.nth("key_side", q - 1))
                            act.wait_ge(b.sem("query_side"), b.nth("query_side", q - 1))
                        for side, sign in zip(range(2), (-INV, INV)):
                            ins = act.activation(sides(ex[:, q % 2, :], z, s)[side], sides(diff[:, q % 2, :], z, s)[side],
                                                 ACT.Exp, scale=sign)
                        ins.then_inc(b.tick("factors_ready"), 1)
                        if h and n == 5:
                            copy_output(h - 1)
                    for z in range(2):
                        u = 2 * h + z
                        act.wait_ge(b.sem("hat_diff"), b.nth("hat_diff", u + 1))
                        if u >= 2:
                            act.wait_ge(b.sem("key_hat"), b.nth("key_hat", u - 1))
                            act.wait_ge(b.sem("query_hat"), b.nth("query_hat", u - 1))
                        last = cum[:, z, h, :].rearrange("p (c r) -> p c r", r=ROW)[:, :, (ROW - 1) * (1 - z)]
                        act.activation(el[:, z, :], last, ACT.Exp, scale=INV)
                        act.activation(ek[:, z, :], hd[:, z, :], ACT.Exp, scale=-INV)
                        act.activation(eq[:, z, :], cum[:, z, h, :], ACT.Exp, scale=INV)\
                            .then_inc(b.tick("hat_factors"), 1)
                    for z in range(2):
                        u = 2 * h + z
                        act.wait_ge(b.sem("key_hat_turned"), b.nth("key_hat_turned", u + 1))
                        if u >= 2:
                            act.wait_ge(b.sem("state_addend"), b.nth("state_addend", (u - 1) * (NCH - 1)))
                        act.activation(kh[:, z, :, :].rearrange("p t k -> p (t k)"), b.psum[:, 6, :], ACT.Copy)\
                            .then_inc(b.tick("key_hat_copied"), 1)
                copy_output(GH - 1)

            @block.gpsimd
            def _(pool):
                for h in range(GH):
                    for n in range(NL):
                        q = h * NL + n
                        z, s = level(n)
                        pool.wait_ge(b.sem("factors_ready"), b.nth("factors_ready", q + 1))
                        if q >= 2:
                            pool.wait_ge(b.sem("score_made"), b.nth("score_made", (q - 2) // NL * NI + (q - 2) % NL + 2))
                        pool.tensor_tensor(sides(kq[:, q % 2, :], z, s)[1], sides(ex[:, q % 2, :], z, s)[1],
                                                 sides(qT[:, h, :], z, s)[1], ALU.mult)\
                                                     .then_inc(b.tick("query_side"), 1)
                    for z in range(2):
                        pool.wait_ge(b.sem("hat_factors"), b.nth("hat_factors", 2 * h + z + 1))
                        if h:
                            pool.wait_ge(b.sem("output_made"), b.nth("output_made", 2 * h))
                        pool.tensor_tensor(qhT[:, z, :], eq[:, z, :], qT[:, h, :], ALU.mult)\
                            .then_inc(b.tick("query_hat"), 1)

            @block.vector
            def _(dve):
                dve.wait_ge(b.sem("masks_in"), b.nth("masks_in", 32))
                dve.tensor_copy(masks[:].rearrange("p n k -> p (n k)"), wide_masks).then_inc(b.tick("masks_ready"), 1)
                dve.wait_ge(b.sem("masks_ready"), b.nth("masks_ready", 1))

                def make_diff(h, n):
                    q = h * NL + n
                    z, s = level(n)
                    if q >= 2:
                        dve.wait_ge(b.sem("factors_ready"), b.nth("factors_ready", q - 1))
                    x = cum[:, z, h, :].rearrange("p (n i) -> p n i", i=2 * s)
                    edge = x[:, :, s - 1 + z:s + z].broadcast_to([P, T // (2 * s), 2 * s])
                    dve.tensor_tensor(diff[:, q % 2, :].rearrange("p (n i) -> p n i", i=2 * s), x, edge,
                                            ALU.subtract).then_inc(b.tick("diff_ready"), 1)

                def make_key_side(h, n):
                    q = h * NL + n
                    z, s = level(n)
                    dve.wait_ge(b.sem("factors_ready"), b.nth("factors_ready", q + 1))
                    if q >= 2:
                        dve.wait_ge(b.sem("score_made"), b.nth("score_made", (q - 2) // NL * NI + (q - 2) % NL + 2))
                    dve.tensor_tensor(sides(kq[:, q % 2, :], z, s)[0], sides(ex[:, q % 2, :], z, s)[0],
                                            sides(kT[:, h, :], z, s)[0], ALU.mult).then_inc(b.tick("key_side"), 1)

                def take_score(h, it):
                    m = h * NI + it
                    dve.wait_ge(b.sem("score_made"), b.nth("score_made", m + 1))
                    made = b.psum[:, 4 + m % 2, :].rearrange("p (t k) -> p t k", t=TT)
                    if it == 0:
                        if h >= 2:
                            dve.wait_ge(b.sem("output_made"), b.nth("output_made", 2 * (h - 1)))
                        ins = dve.tensor_tensor(score[:, h % 2], made, diag2[:].unsqueeze(1).broadcast_to([P, TT, P]),
                                                ALU.mult)
                    else:
                        dve.wait_ge(b.sem("score_taken"), b.nth("score_taken", m))
                        ins = dve.copy_predicated(score[:, h % 2],
                                                  masks[:, it - 1, :].unsqueeze(1).broadcast_to([P, TT, P]), made)
                    ins.then_inc(b.tick("score_taken"), 1)

                for h in range(GH):
                    make_diff(h, 0)
                    for n in range(NL):
                        if n + 1 < NL:
                            make_diff(h, n + 1)
                        make_key_side(h, n)
                        take_score(h, n)
                    take_score(h, NL)
                    for z in range(2):
                        u = 2 * h + z
                        if u >= 2:
                            dve.wait_ge(b.sem("hat_factors"), b.nth("hat_factors", u - 1))
                        x = cum[:, z, h, :].rearrange("p (c r) -> p c r", r=ROW)
                        e = (ROW - 1) * (1 - z)
                        dve.tensor_tensor(hd[:, z, :].rearrange("p (c r) -> p c r", r=ROW), x,
                                                x[:, :, e:e + 1].broadcast_to([P, NCH, ROW]), ALU.subtract)\
                                                    .then_inc(b.tick("hat_diff"), 1)
                    for z in range(2):
                        u = 2 * h + z
                        dve.wait_ge(b.sem("hat_factors"), b.nth("hat_factors", u + 1))
                        if u >= 2:
                            dve.wait_ge(b.sem("key_hat_turned"), b.nth("key_hat_turned", u - 1))
                        dve.tensor_tensor(khT[:, z, :], ek[:, z, :], kT[:, h, :], ALU.mult)\
                            .then_inc(b.tick("key_hat"), 1)
                    if h:
                        dve.wait_ge(b.sem("output_made"), b.nth("output_made", 2 * h))
                    for z in range(2):
                        for i, c in enumerate(scan_order(z)[:-1]):
                            x = (2 * h + z) * (NCH - 1) + i
                            dve.wait_ge(b.sem("state_addend"), b.nth("state_addend", x + 1))
                            add = b.psum[:, 2 + x % 2, 0:GDV]
                            if i == 0:
                                ins = dve.tensor_copy(state[:, z, 0, :], add)
                            else:
                                dve.wait_ge(b.sem("state_ready"), b.nth("state_ready", x))
                                ins = dve.scalar_tensor_tensor(state[:, z, i, :], state[:, z, i - 1, :],
                                                               el[:, z, c:c + 1], add, ALU.mult, ALU.add)
                            ins.then_inc(b.tick("state_ready"), 1)


def gla_out(b, oT, gate):
    st = ExitStack()
    with st:
        input_parts(b, st)
        sq = b.sb(st, "gla_sq", [P, 2, T])
        rstd = b.sb(st, "gla_rstd", [P, 2, T])
        with b.stage() as block:
            w0, _, wt, _ = b.phases["gla_out"]

            @block.sync
            def _(sp):
                b.stream(sp, "gla_out")

            @block.gpsimd
            def _(pool):
                for m in range(KD):
                    if m >= 2:
                        pool.wait_ge(b.sem("square_added"), b.nth("square_added", m - 1))
                    pool.tensor_tensor(sq[:, m % 2, :], oT[:, m, :], oT[:, m, :], ALU.mult)\
                        .then_inc(b.tick("squared"), 1)
                for m in range(KD):
                    pool.wait_ge(b.sem("normed"), b.nth("normed", m + 1))
                    raw_free(b, pool, m)
                    pool.tensor_tensor(b.raw[:, m % 2, :], oT[:, m, :], gate[:, m, :], ALU.mult).then_inc(b.tick("modulated"), 1)

            @block.tensor
            def _(pe):
                for m in range(KD):
                    pe.wait_ge(b.sem("squared"), b.nth("squared", m + 1))
                    pe.matmul(b.psum[:, 4 + m // 2, :], b.ones[:], sq[:, m % 2, :], start=m % 2 == 0,
                                    stop=m % 2 == 1).then_inc(b.tick("square_added"), 1)
                pe.wait_ge(b.sem("input_split"), b.nth("input_split", KD))
                for j in range(KD):
                    b.products(pe, "gla_out", j, ALL, b.input(ALL))

            @block.scalar
            def _(act):
                b.round_weights(act, w0 + 1)
                for h in range(GH):
                    act.wait_ge(b.sem("square_added"), b.nth("square_added", 2 * h + 2))
                    if h >= 2:
                        act.wait_ge(b.sem("normed"), b.nth("normed", 2 * (h - 1)))
                    act.activation(rstd[:, h % 2, :], b.psum[:, 4 + h, :], ACT.Sqrt, bias=b.eps[:, 1:2],
                                         scale=1.0 / GDV).then_inc(b.tick("deviation_ready"), 1)
                for k in range(KD):
                    round_input(b, act, k, ALL)
                b.round_weights(act, w0 + KD - 1 + AHEAD)

            @block.vector
            def _(dve):
                b.split_weights(dve, "dve", w0 + 1)
                for h in range(GH):
                    dve.wait_ge(b.sem("deviation_ready"), b.nth("deviation_ready", h + 1))
                    dve.reciprocal(rstd[:, h % 2, :], rstd[:, h % 2, :]).then_inc(b.tick("dve_step"), 1)
                    dve.wait_ge(b.sem("dve_step"), b.all("dve_step"))
                    for vt in range(2):
                        m = 2 * h + vt
                        dve.scalar_tensor_tensor(oT[:, m, :], oT[:, m, :], column(b, C_GLAN, vt),
                                                       rstd[:, h % 2, :], ALU.mult, ALU.mult)\
                                                           .then_inc(b.tick("normed"), 1)
                for k in range(KD):
                    split_input(b, dve, k, ALL)
                for m in range(KD):
                    residual(b, dve, 0, 2, ALL, wt + m, m)


def ssd_layer(b):
    st = ExitStack()
    with st:
        xs = b.sb(st, "ssd_x", [P, TT, SDI])
        bt = b.sb(st, "ssd_b", [P, TT, SG * SN])
        bT, cT = b.H2[:, :, NCTX:T], b.H1[:, :, 0:NCTX]
        z = b.sb(st, "ssd_z", [P, SDI // P, NLAT])
        y = xs[:, 0:2, :]
        s = b.sb(st, "ssd_state", [P, 2, SDI])
        cum = b.sb(st, "ssd_cum", [2 * SH, T])
        tok = b.sb(st, "ssd_tok", [P, 10, 2 * SH])
        el = b.sb(st, "ssd_el", [P, NCH, 2, SH])
        dskip = b.sb(st, "ssd_dskip", [P, SH])
        causal = b.sb(st, "ssd_causal", [P, 2, P])
        ssd_project(b, xs, bt, bT, cT, z, s, cum, tok, el, dskip, causal)
        ssd_states(b, xs, bt, cT, y, s, tok, el, dskip)
        ssd_intra(b, xs, bT, cT, y, s, cum, tok, causal)
        ssd_out(b, xs, z, y)


def ssd_project(b, xs, bt, bT, cT, z, s, cum, tok, el, dskip, causal):
    d = b.dram
    R = 2 * SH
    dx, de, dt, dta, wt, ec, rep = (s[0:R, i // 4, (i % 4) * T:(i % 4 + 1) * T] for i in range(7))
    NC = 4
    NX, NB = SDI // P, SDI // P + SG
    st = ExitStack()
    with st:
        conv = b.sb(st, "ssd_conv", [P, NC, T])
        input_parts(b, st, conv[:, 0:2, :])
        small = b.sb(st, "ssd_small", [R, 1 + NCH])
        with b.stage() as block:
            d0, _, dtile, _ = b.phases["ssd_dt"]
            z0, _, zt, zn = b.phases["ssd_z"]
            x0, _, xt, xn = b.phases["ssd_xbc"]

            @block.sync
            def _(sp):
                sp.dma_start(dskip[:], d["ssd_d"][0:1, :].broadcast_to([P, SH]))\
                    .then_inc(b.tick("scan_constants_in", 16), 16)
                sp.dma_start(causal[:], d["c_causal"]).then_inc(b.tick("scan_constants_in", 16), 16)
                sp.dma_start(rep[:], d["c_reset"][0:R, :]).then_inc(b.tick("scan_constants_in", 16), 16)
                for phase in ("ssd_dt", "ssd_z", "ssd_xbc"):
                    b.stream(sp, phase)

            @block.tensor
            def _(pe):
                pe.wait_ge(b.sem("input_split"), b.nth("input_split", KD))
                b.products(pe, "ssd_dt", 0, ALL, b.input(ALL))
                for m in range(zn):
                    b.products(pe, "ssd_z", m, LAT, b.input(LAT))

                def turn(m):
                    pe.wait_ge(b.sem("activated"), b.nth("activated", m + 1))
                    if m >= 4:
                        pe.wait_ge(b.sem("tokens_copied"), b.nth("tokens_copied", m - 3))
                    for t in range(TT):
                        ins = pe.transpose(b.psum[:, 4 + m % 4, t * P:(t + 1) * P],
                                           conv[:, m % NC, t * P:(t + 1) * P], b.ident[:])
                    ins.then_inc(b.tick("tokens_turned"), 1)

                for m in range(xn):
                    cols = ALL if m < NB else LAT
                    b.products(pe, "ssd_xbc", m, cols, b.input(cols))
                    if 2 <= m < NB + 2:
                        turn(m - 2)
                pe.wait_ge(b.sem("decays_ready"), b.nth("decays_ready", 1))
                pe.wait_ge(b.sem("tokens_copied"), b.nth("tokens_copied", NB))
                for i, (src, t) in enumerate([(x, t) for x in (cum, dt, ec) for t in (2, 3)] + [(wt, t) for t in range(TT)]):
                    ins = pe.transpose(b.psum[:, 4 + i // 8, i % 8 * R:(i % 8 + 1) * R], src[:, t * P:(t + 1) * P],
                                       b.ident[0:R, 0:R])
                pe.matmul(b.psum[:, 6, :], b.ones[0:R, :], dx[:], start=True, stop=True)\
                    .then_inc(b.tick("decays_turned"), 1)

            @block.gpsimd
            def _(pool):
                b.split_weights(pool, "pool", x0 + xn - 1)

            @block.scalar
            def _(act):

                def step(*a, **k):
                    act.activation(*a, **k).then_inc(b.tick("act_step"), 1)
                    act.wait_ge(b.sem("act_step"), b.all("act_step"))

                b.round_weights(act, d0)
                for k in range(KD):
                    round_input(b, act, k, ALL)
                b.round_weights(act, d0 + AHEAD)
                act.wait_ge(b.sem("product_done"), dtile + 1)
                act.activation(dx[:], b.bank(dtile)[P - R:P, :], ACT.Copy).then_inc(b.reads_out(dtile), 1)
                act.wait_ge(*b.evacuated(dtile))
                step(dx[:], dx[:], ACT.Identity, bias=column(b, C_DTB, 0, R))
                step(de[:], dx[:], ACT.Abs)
                step(de[:], de[:], ACT.Exp, scale=-1.0)
                step(small[:, 0:1], column(b, C_ALOG, 0, R), ACT.Exp)
                act.activation(de[:], de[:], ACT.Ln, bias=1.0).then_inc(b.tick("softplus_ready"), 1)
                for m in range(zn):
                    b.round_weights(act, b.last_slot(zt + m) + AHEAD)
                    act.wait_ge(b.sem("product_done"), zt + m + 1)
                    act.activation(z[:, m, :], b.bank(zt + m)[:, NCTX:T], ACT.Silu).then_inc(b.reads_out(zt + m), 1)
                act.wait_ge(b.sem("cum_ready"), b.nth("cum_ready", 1))
                act.activation(ec[:], cum[:], ACT.Exp)
                for q, e in ((0, ROW - 1), (1, 0)):
                    rows = slice(SH * q, SH * (q + 1))
                    act.activation(small[rows, 1:], cum[rows, :].rearrange("p (c r) -> p c r", r=ROW)[:, :, e], ACT.Exp)
                act.activation(wt[:], wt[:], ACT.Exp, scale=-1.0).then_inc(b.tick("decay_factors"), 1)

                def copy(m):
                    act.wait_ge(b.sem("tokens_turned"), b.nth("tokens_turned", m + 1))
                    dst = xs[:, :, m * P:(m + 1) * P] if m < NX else bt[:, :, (m - NX) * P:(m - NX + 1) * P]
                    act.activation(dst, b.psum[:, 4 + m % 4, :].rearrange("p (t f) -> p t f", t=TT), ACT.Copy)\
                        .then_inc(b.tick("tokens_copied"), 1)

                for m in range(xn):
                    b.round_weights(act, b.last_slot(xt + m) + AHEAD)
                    act.wait_ge(*b.evacuated(xt + m))
                    c = conv[:, m % NC, :]
                    if m >= NB:
                        act.activation(cT[:, m - NB, :], c[:, NCTX:T], ACT.Silu).then_inc(b.tick("c_activated"), 1)
                    else:
                        if m >= NX:
                            step(bT[:, m - NX, :], c[:, NCTX:T], ACT.Silu)
                        act.activation(c, c, ACT.Silu).then_inc(b.tick("activated"), 1)
                    if 2 <= m < NB + 2:
                        copy(m - 2)

            @block.vector
            def _(dve):

                def step(ins):
                    ins.then_inc(b.tick("dve_step"), 1)
                    dve.wait_ge(b.sem("dve_step"), b.all("dve_step"))

                modulate(b, dve, 1, 0, ALL)
                dve.wait_ge(b.sem("scan_constants_in"), b.nth("scan_constants_in", 48))
                dve.wait_ge(b.sem("softplus_ready"), b.nth("softplus_ready", 1))
                step(dve.scalar_tensor_tensor(dt[:], dx[:], 0.0, de[:], ALU.max, ALU.add))
                step(dve.tensor_scalar(dta[:], dt[:], small[:, 0:1], -1.0, ALU.mult, ALU.mult))
                f, r = slice(0, SH), slice(SH, R)
                dve.tensor_tensor_scan(cum[f, :], rep[f, :], dta[f, :], 0.0, ALU.mult, ALU.add)\
                    .then_inc(b.tick("dve_step"), 1)
                step(dve.tensor_tensor_scan(cum[r, ::-1], rep[r, :], dta[r, ::-1], 0.0, ALU.mult, ALU.add))
                for rows, e in ((f, ROW - 1), (r, 0)):
                    x = cum[rows, :].rearrange("p (c r) -> p c r", r=ROW)
                    ins = dve.tensor_tensor(wt[rows, :].rearrange("p (c r) -> p c r", r=ROW), x,
                                            x[:, :, e:e + 1].broadcast_to([SH, NCH, ROW]), ALU.subtract)
                    if e:
                        ins.then_inc(b.tick("dve_step"), 1)
                    else:
                        ins.then_inc(b.tick("cum_ready"), 1)

                def conv_tile(m):
                    dve.wait_ge(b.sem("product_done"), xt + m + 1)
                    if NC <= m < NB + NC:
                        dve.wait_ge(b.sem("tokens_turned"), b.nth("tokens_turned", m - NC + 1))
                    elif m >= NB + NC:
                        dve.wait_ge(b.sem("c_activated"), b.nth("c_activated", m - NC - NB + 1))
                    segs = 2 if m < NB else 1
                    c0 = T - segs * NLAT
                    src = b.bank(xt + m)[:, c0:T].rearrange("p (s t) -> p s t", s=segs)
                    dst = conv[:, m % NC, c0:T].rearrange("p (s t) -> p s t", s=segs)

                    def tap(k):
                        return column(b, C_CONVW, 32 * k + m)

                    mid = SCONV // 2
                    step(dve.tensor_scalar(dst, src, tap(mid), column(b, C_CONVB, m), ALU.mult, ALU.add))
                    for k in (0, 1, 3, 4):
                        off = k - mid
                        o, i = (slice(-off, NLAT), slice(0, NLAT + off)) if off < 0 else (slice(0, NLAT - off), slice(off, NLAT))
                        ins = dve.scalar_tensor_tensor(dst[:, :, o], src[:, :, i], tap(k), dst[:, :, o], ALU.mult, ALU.add)
                        if k < 4:
                            step(ins)
                        else:
                            ins.then_inc(b.reads_out(xt + m), 1)

                for m in range(4):
                    conv_tile(m)
                dve.wait_ge(b.sem("decay_factors"), b.nth("decay_factors", 1))
                step(dve.tensor_tensor(wt[:], wt[:], dt[:], ALU.mult))
                dve.tensor_tensor(dx[:].rearrange("p (c r) -> p c r", c=NCH),
                                        b.ident[0:R, 0:R].unsqueeze(1).broadcast_to([R, NCH, R]),
                                        small[:, 1:].unsqueeze(2).broadcast_to([R, NCH, R]), ALU.mult)\
                                            .then_inc(b.tick("decays_ready"), 1)
                for m in range(4, xn):
                    conv_tile(m)
                dve.wait_ge(b.sem("decays_turned"), b.nth("decays_turned", 1))
                dve.tensor_copy(tok[:, 0:8, :].rearrange("p a r -> p (a r)"), b.psum[:, 4, :])
                dve.tensor_copy(tok[:, 8:10, :].rearrange("p a r -> p (a r)"), b.psum[:, 5, 0:2 * R])
                dve.tensor_copy(el[:].rearrange("p c z h -> p (c z h)"), b.psum[:, 6, :])


def ssd_states(b, xs, bt, cT, y, s, tok, el, dskip):
    seq = [(i, z, scan_order(z)[i]) for i in range(NCH) for z in range(2)]
    HB = [SG, SREP, SHD]

    def heads(ap):
        return ap.rearrange("p g (r w) -> p g r w", w=SHD)

    def spread(ap):
        n = ap.shape[0]
        return ap.unsqueeze(2).broadcast_to([n, SH, SHD])

    def flat(ap):
        return ap.rearrange("p (h w) -> p h w", w=SHD)

    before = [x for x in seq if x[0] >= NCH // 2]
    st = ExitStack()
    with st:
        weighted = [b.sb(st, "ssd_weighted", [P, SG, SREP * SHD]) for _ in range(2)]
        part = b.sb(st, "ssd_part", [P, SG, SREP * SHD])
        with b.stage() as block:

            @block.tensor
            def _(pe):
                inter = upd = 0
                for i, z, c in seq:
                    rows = slice(ROW * (c % 2), ROW * (c % 2) + ROW)
                    if i >= NCH // 2:
                        pe.wait_ge(b.sem("state_ready"), b.nth("state_ready", 2 * (i - 1) + z + 1))
                        if inter:
                            pe.wait_ge(b.sem("part_scaled"), b.nth("part_scaled", inter))
                        lc = (c - NCH // 2) * ROW
                        for g in range(SG):
                            ins = pe.matmul(b.psum[rows, g // 2, 256 * (g % 2):256 * (g % 2) + 256], cT[:, g, lc:lc + ROW],
                                            s[:, z, 256 * g:256 * g + 256], start=g % 2 == 0, stop=g % 2 == 1,
                                            skip_group_check=True)
                        ins.then_inc(b.tick("part_made"), 1)
                        inter += 1
                    if i < NCH - 1:
                        pe.wait_ge(b.sem("weighted_ready"), b.nth("weighted_ready", (i // 2) * 2 + z + 1))
                        if upd:
                            pe.wait_ge(b.sem("state_ready"), b.nth("state_ready", upd))
                        for g in range(SG):
                            ins = pe.matmul(b.psum[:, 4 + g // 2, 256 * (g % 2):256 * (g % 2) + 256],
                                            bt[rows, c // 2, g * SN:(g + 1) * SN], weighted[z][rows, g, :],
                                            start=g % 2 == 0, stop=g % 2 == 1, skip_group_check=True)
                        ins.then_inc(b.tick("addend_made"), 1)
                        upd += 1

            @block.gpsimd
            def _(pool):
                for i in range(0, NCH, 2):
                    for z in range(2):
                        t = scan_order(z)[i] // 2
                        if i:
                            pool.wait_ge(b.sem("addend_made"), b.nth("addend_made", 2 * (i - 1) + z + 1))
                        ins = pool.tensor_tensor(heads(weighted[z][:]), xs[:, t, :].rearrange("p (g r w) -> p g r w", g=SG, w=SHD),
                                                 tok[:, 6 + t, z * SH:(z + 1) * SH].rearrange("p (g r) -> p g r", g=SG)
                                                 .unsqueeze(3).broadcast_to([P, SG, SREP, SHD]), ALU.mult)
                        ins.then_inc(b.tick("weighted_ready"), 1)
                    if i == NCH // 2 - 2:
                        pool.wait_ge(b.sem("weighted_ready"), b.all("weighted_ready"))
                        for t in range(2):
                            ins = pool.tensor_tensor(flat(y[:, t, :]), flat(xs[:, 2 + t, :]), spread(dskip[:]), ALU.mult)
                        ins.then_inc(b.tick("skip_ready"), 1)

            @block.vector
            def _(dve):
                inter = upd = 0
                psum = b.psum[:].rearrange("p b n -> p (b n)")
                for i, z, c in seq:
                    rows = slice(ROW * (c % 2), ROW * (c % 2) + ROW)
                    if i >= NCH // 2:
                        inter += 1
                        if inter == 1:
                            dve.wait_ge(b.sem("skip_ready"), b.nth("skip_ready", 1))
                        dve.wait_ge(b.sem("part_made"), b.nth("part_made", inter))
                        t = c // 2 - 2
                        dve.wait_ge(b.sem("dve_step"), b.all("dve_step"))
                        dve.tensor_tensor(part[rows].rearrange("p g (r w) -> p g r w", w=SHD),
                                                psum[rows, 0:SDI].rearrange("p (g r w) -> p g r w", g=SG, w=SHD),
                                                tok[rows, 4 + t, z * SH:(z + 1) * SH].rearrange("p (g r) -> p g r", g=SG)
                                                .unsqueeze(3).broadcast_to([ROW, SG, SREP, SHD]), ALU.mult)\
                                                    .then_inc(b.tick("part_scaled"), 1)
                        dve.wait_ge(b.sem("part_scaled"), b.nth("part_scaled", inter))
                        yv = y[rows, t, :].rearrange("p (g n) -> p g n", g=SG)
                        dve.tensor_tensor(yv, yv, part[rows], ALU.add).then_inc(b.tick("dve_step"), 1)
                    if i < NCH - 1:
                        upd += 1
                        if i:
                            dve.wait_ge(b.sem("state_ready"), b.nth("state_ready", upd - 1))
                            if i >= NCH // 2:
                                dve.wait_ge(b.sem("part_made"), b.nth("part_made", inter))
                            dve.tensor_tensor(flat(s[:, z, :]), flat(s[:, z, :]), spread(el[:, c, z, :]), ALU.mult)\
                                .then_inc(b.tick("dve_step"), 1)
                            dve.wait_ge(b.sem("dve_step"), b.all("dve_step"))
                            dve.wait_ge(b.sem("addend_made"), b.nth("addend_made", upd))
                            ins = dve.tensor_tensor(s[:, z, :], s[:, z, :], psum[:, SDI:2 * SDI], ALU.add)
                        else:
                            dve.wait_ge(b.sem("addend_made"), b.nth("addend_made", upd))
                            ins = dve.tensor_copy(s[:, z, :], psum[:, SDI:2 * SDI])
                        ins.then_inc(b.tick("state_ready"), 1)


def ssd_intra(b, xs, bT, cT, y, state, cum, tok, causal):
    cbm = state[:, 0, 0:8 * P].rearrange("p (b z t i) -> p b z t i", b=2, z=2, t=2)
    st = ExitStack()
    with st:
        seg = [b.sb(st, "ssd_seg", [P, 2 * SREP, NLAT]) for _ in range(2)]
        with b.stage() as block:

            def head(q, g):
                return q // SREP * SH + g * SREP + q % SREP

            @block.tensor
            def _(pe):
                def scores(g):
                    if g >= 2:
                        pe.wait_ge(b.sem("scores_masked"), b.nth("scores_masked", 2 * (g - 1)))
                    for t in range(2):
                        ins = pe.matmul(b.psum[:, 4 + g % 2, t * P:(t + 1) * P], bT[:, g, t * P:(t + 1) * P],
                                        cT[:, g, t * P:(t + 1) * P], start=t == 0, stop=t == 1, skip_group_check=True)
                    ins.then_inc(b.tick("scores_made"), 1)
                    if g:
                        pe.wait_ge(b.sem("segments_ready"), b.nth("segments_ready", g))
                    for q in range(2 * SREP):
                        row = head(q, g)
                        ins = pe.matmul(b.psum[:, q // 2, 256 * (q % 2):256 * (q % 2) + 256],
                                        b.ident[0:2 * SH, row:row + 1].broadcast_to([2 * SH, P]), cum[:, NCTX:T],
                                        start=q % 2 == 0, stop=q % 2 == 1, skip_group_check=True)
                    ins.then_inc(b.tick("rows_spread"), 1)

                def mix(g):
                    pe.wait_ge(b.sem("mixes_ready"), b.nth("mixes_ready", g + 1))
                    if g >= 2:
                        pe.wait_ge(b.sem("mixed_added"), b.nth("mixed_added", g - 1))
                    n = 0
                    for t in range(2):
                        for r in range(SREP):
                            for z in range(2):
                                h = g * SREP + r
                                ins = pe.matmul(b.psum[:, 6 + g % 2, t * 256 + r * SHD:t * 256 + (r + 1) * SHD],
                                                seg[g % 2][:, z * SREP + r, t * P:(t + 1) * P],
                                                xs[:, 2 + t, h * SHD:(h + 1) * SHD], start=n == 0, stop=n == 15,
                                                skip_group_check=True)
                                n += 1
                    ins.then_inc(b.tick("mixed"), 1)

                scores(0)
                for g in range(SG):
                    if g + 1 < SG:
                        scores(g + 1)
                    mix(g)

            @block.scalar
            def _(act):
                for g in range(SG):
                    act.wait_ge(b.sem("segments_ready"), b.nth("segments_ready", g + 1))
                    act.activation(seg[g % 2][:], seg[g % 2][:], ACT.Exp).then_inc(b.tick("decays_ready"), 1)

            @block.vector
            def _(dve):
                def segments(g):
                    dve.wait_ge(b.sem("scores_made"), b.nth("scores_made", g + 1))
                    if g >= 2:
                        dve.wait_ge(b.sem("mixed"), b.nth("mixed", g - 1))
                    for z in range(2):
                        dve.tensor_tensor(cbm[:, g % 2, z], b.psum[:, 4 + g % 2, 0:256].rearrange("p (t i) -> p t i", t=2),
                                                causal[:, z, :].unsqueeze(1).broadcast_to([P, 2, P]), ALU.mult)\
                                                    .then_inc(b.tick("scores_masked"), 1)
                    dve.wait_ge(b.sem("rows_spread"), b.nth("rows_spread", g + 1))
                    for q in range(2 * SREP):
                        for t in range(2):
                            ins = dve.tensor_scalar(seg[g % 2][:, q, t * P:(t + 1) * P],
                                                    b.psum[:, q // 2, 256 * (q % 2) + t * P:256 * (q % 2) + (t + 1) * P],
                                                    tok[:, t, head(q, g):head(q, g) + 1], 0.0, ALU.subtract, ALU.min)
                    ins.then_inc(b.tick("segments_ready"), 1)

                segments(0)
                for g in range(SG):
                    if g + 1 < SG:
                        segments(g + 1)
                    dve.wait_ge(b.sem("decays_ready"), b.nth("decays_ready", g + 1))
                    dve.wait_ge(b.sem("scores_masked"), b.nth("scores_masked", 2 * (g + 1)))
                    for q in range(2 * SREP):
                        for t in range(2):
                            m = seg[g % 2][:, q, t * P:(t + 1) * P]
                            ins = dve.scalar_tensor_tensor(m, m, tok[:, 2 + t, head(q, g):head(q, g) + 1],
                                                           cbm[:, g % 2, q // SREP, t, :], ALU.mult, ALU.mult)
                    ins.then_inc(b.tick("mixes_ready"), 1)
                    if g:
                        add_mixed(b, dve, y, g - 1)
                add_mixed(b, dve, y, SG - 1)


def add_mixed(b, dve, y, g):
    dve.wait_ge(b.sem("mixed"), b.nth("mixed", g + 1))
    v = y[:, :, g * 256:(g + 1) * 256]
    dve.tensor_tensor(v, v, b.psum[:, 6 + g % 2, :].rearrange("p (t n) -> p t n", t=2), ALU.add)\
        .then_inc(b.tick("mixed_added"), 1)


def ssd_out(b, xs, z, y):
    NF = SDI // P
    yT = xs[:, 2:4, :].rearrange("p a (f t) -> p (a f) t", t=NLAT)
    st = ExitStack()
    with st:
        sq = b.sb(st, "ssd_sq", [P, 2, NLAT])
        rstd = b.sb(st, "ssd_rstd", [P, NLAT])
        yh = b.sb(st, "ssd_out_hi", [P, NF, NLAT])
        yl = b.sb(st, "ssd_out_lo", [P, NF, NLAT])
        yh_r, yl_r = yh[:].bitcast(F32R), yl[:].bitcast(F32R)
        ssd_out_stage(b, z, y, yT, sq, rstd, yh, yh_r, yl_r)


def ssd_out_stage(b, z, y, yT, sq, rstd, yh, yh_r, yl_r):
    NF = SDI // P
    with b.stage() as block:
        w0, _, wt, wn = b.phases["ssd_out"]

        @block.sync
        def _(sp):
            b.stream(sp, "ssd_out")

        @block.tensor
        def _(pe):
            def add_square(f):
                pe.wait_ge(b.sem("squared"), b.nth("squared", f + 1))
                pe.matmul(b.psum[:, 4, 0:NLAT], b.ones[:], sq[:, f % 2, :], start=f == 0, stop=f == NF - 1)\
                    .then_inc(b.tick("square_added"), 1)

            for f in range(NF):
                if f >= 3:
                    pe.wait_ge(b.sem("gated"), b.nth("gated", f - 2))
                for t in range(2):
                    ins = pe.transpose(b.psum[:, 5 + f % 3, t * P:(t + 1) * P], y[:, t, f * P:(f + 1) * P], b.ident[:])
                ins.then_inc(b.tick("feature_turned"), 1)
                if f >= 2:
                    add_square(f - 2)
            add_square(NF - 2)
            add_square(NF - 1)
            for s in range(2 * wn):
                k0 = s % 2 * KD
                pe.wait_ge(b.sem("output_split"), b.nth("output_split", k0 + KD))
                pe.wait_ge(*b.weights_split(w0 + s))
                b.product(pe, wt + s // 2, lambda x: x[:, NCTX:T],
                          b.passes(w0 + s, slice(0, P), lambda k: (yh_r[:, k0 + k, :], yl_r[:, k0 + k, :])),
                          first=s % 2 == 0, last=s % 2 == 1)

        @block.gpsimd
        def _(pool):
            for f in range(NF):
                pool.wait_ge(b.sem("gated"), b.nth("gated", f + 1))
                if f >= 2:
                    pool.wait_ge(b.sem("square_added"), b.nth("square_added", f - 1))
                pool.tensor_tensor(sq[:, f % 2, :], yT[:, f, :], yT[:, f, :], ALU.mult).then_inc(b.tick("squared"), 1)

        @block.scalar
        def _(act):
            b.round_weights(act, w0 + 1)
            act.wait_ge(b.sem("square_added"), b.nth("square_added", NF))
            act.activation(rstd[:], b.psum[:, 4, 0:NLAT], ACT.Sqrt, bias=b.eps[:, 1:2], scale=1.0 / SDI)\
                .then_inc(b.tick("deviation_ready"), 1)
            for f in range(NF):
                act.wait_ge(b.sem("normed"), b.nth("normed", f + 1))
                act.activation(yh_r[:, f, :], yT[:, f, :], ACT.Copy).then_inc(b.tick("output_rounded"), 1)
            b.round_weights(act, w0 + 2 * wn - 1 + AHEAD)

        @block.vector
        def _(dve):
            def split_output(f):
                dve.wait_ge(b.sem("output_rounded"), b.nth("output_rounded", f + 1))
                dve.tensor_tensor(yl_r[:, f, :], yT[:, f, :], yh[:, f, :], ALU.subtract)\
                    .then_inc(b.tick("output_split"), 1)

            b.split_weights(dve, "dve", w0 + 1)
            for f in range(NF):
                dve.wait_ge(b.sem("feature_turned"), b.nth("feature_turned", f + 1))
                dve.tensor_tensor(yT[:, f, :], b.psum[:, 5 + f % 3, 0:NLAT], z[:, f, :], ALU.mult)\
                    .then_inc(b.tick("gated"), 1)
            dve.wait_ge(b.sem("deviation_ready"), b.nth("deviation_ready", 1))
            dve.reciprocal(rstd[:], rstd[:]).then_inc(b.tick("dve_step"), 1)
            dve.wait_ge(b.sem("dve_step"), b.all("dve_step"))
            dve.wait_ge(b.sem("squared"), b.nth("squared", NF))
            for f in range(NF):
                dve.scalar_tensor_tensor(yT[:, f, :], yT[:, f, :], column(b, C_SSDN, f), rstd[:], ALU.mult, ALU.mult)\
                    .then_inc(b.tick("normed"), 1)
                if f >= 2:
                    split_output(f - 2)
            split_output(NF - 2)
            split_output(NF - 1)
            for m in range(wn):
                residual(b, dve, 1, 2, LAT, wt + m, m)


def attention_layer(b, l):
    last = l == DEPTH - 1
    seg = LAT if last else ALL
    st = ExitStack()
    with st:
        input_parts(b, st, raw=False)
        o = b.sb(st, "att_o", [P, 3, BW // P, T])
        heads = ExitStack()
        with heads:
            m = {"q": b.sb(heads, "att_q", [P, 8, T]), "k": b.sb(heads, "att_k", [P, 8, T]),
                 "v": b.sb(heads, "att_v", [P, TT, BW]),
                 "z": b.sb(heads, "att_z", [P, BW // P, T]), "o": o}
            input_norm(b, l)
            project_heads(b, l, "na", seg, m)
            attend(b, l, 0, m, last)
            project_latent(b, l, seg, m)
            attend(b, l, 1, m, last)
            project_heads(b, l, "diff", seg, m)
            attend(b, l, 2, m, last)
        merge(b, l, seg, o)


def input_norm(b, l):
    st = ExitStack()
    with st:
        sq = b.sb(st, "in_sq", [P, 2, T])
        rstd = b.sb(st, "in_rstd", [P, T])
        b.raw = b.sb(st, "in_raw", [P, 2, T])
        with b.stage() as block:

            @block.tensor
            def _(pe):
                for k in range(KD):
                    pe.wait_ge(b.sem("squared"), b.nth("squared", k + 1))
                    pe.matmul(b.psum[:, 4, :], b.ones[:], sq[:, k % 2, :], start=k == 0, stop=k == KD - 1)\
                        .then_inc(b.tick("square_added"), 1)

            @block.scalar
            def _(act):
                for k in range(KD):
                    if k >= 2:
                        act.wait_ge(b.sem("square_added"), b.nth("square_added", k - 1))
                    act.activation(sq[:, k % 2, :], b.H2[:, k, :], ACT.Square).then_inc(b.tick("squared"), 1)
                b.round_weights(act, b.phases[f"na_qk{l}"][0] + 1)
                act.wait_ge(b.sem("square_added"), b.nth("square_added", KD))
                act.activation(rstd[:], b.psum[:, 4, :], ACT.Sqrt, bias=b.eps[:, 1:2], scale=1.0 / D)\
                    .then_inc(b.tick("deviation_ready"), 1)
                for k in range(KD):
                    round_input(b, act, k, ALL)

            @block.vector
            def _(dve):
                dve.wait_ge(b.sem("deviation_ready"), b.nth("deviation_ready", 1))
                dve.reciprocal(rstd[:], rstd[:]).then_inc(b.tick("dve_step"), 1)
                dve.wait_ge(b.sem("dve_step"), b.all("dve_step"))
                for k in range(KD):
                    raw_free(b, dve, k)
                    x = b.raw[:, k % 2, :]
                    dve.tensor_tensor(x, b.H2[:, k, :], rstd[:], ALU.mult).then_inc(b.tick("dve_step"), 1)
                    if k:
                        split_input(b, dve, k - 1, ALL)
                    dve.wait_ge(b.sem("dve_step"), b.all("dve_step"))
                    for v, (a, e) in enumerate((LAT, CTX)):
                        ins = dve.tensor_scalar(x[:, a:e], x[:, a:e], b.mod2[:, l, KD + k, v:v + 1],
                                                b.mod2[:, l, k, v:v + 1], ALU.mult, ALU.add)
                    ins.then_inc(b.tick("modulated"), 1)
                split_input(b, dve, KD - 1, ALL)

            @block.gpsimd
            def _(pool):
                b.split_weights(pool, "pool", b.phases[f"na_qk{l}"][0] + 1)


def sum_for_norm(b, pe, n, ones, sq, cols):
    rows = ones.shape[0]
    pe.wait_ge(b.sem("squared"), b.nth("squared", n + 1))
    if n >= 2:
        pe.wait_ge(b.sem("deviation_ready"), b.nth("deviation_ready", n - 1))
    w = cols[1] - cols[0]
    pe.matmul(b.psum[0:rows, 4 + n % 2, 0:w], ones, sq[0:rows, n % 2, 0:w], start=True, stop=True)\
        .then_inc(b.tick("square_added"), 1)


def square_for_norm(b, pool, n, g, x, sq, rows, cols):
    pool.wait_ge(*b.evacuated(g))
    if n >= 2:
        pool.wait_ge(b.sem("square_added"), b.nth("square_added", n - 1))
    w = cols[1] - cols[0]
    pool.tensor_tensor(sq[0:rows, n % 2, 0:w], x, x, ALU.mult).then_inc(b.tick("squared"), 1)


def deviation_for_norm(b, act, n, rstd, rows, cols, width):
    act.wait_ge(b.sem("square_added"), b.nth("square_added", n + 1))
    if n >= 2:
        act.wait_ge(b.sem("normed"), b.nth("normed", n - 1))
    w = cols[1] - cols[0]
    act.activation(rstd[0:rows, n % 2, 0:w], b.psum[0:rows, 4 + n % 2, 0:w], ACT.Sqrt,
                         bias=b.eps[0:rows, 1:2], scale=1.0 / width).then_inc(b.tick("deviation_ready"), 1)


def scale_for_norm(b, dve, n, x, rstd, rows, cols, gain):
    w = cols[1] - cols[0]
    r = rstd[0:rows, n % 2, 0:w]
    dve.wait_ge(b.sem("deviation_ready"), b.nth("deviation_ready", n + 1))
    dve.reciprocal(r, r).then_inc(b.tick("dve_step"), 1)
    dve.wait_ge(b.sem("dve_step"), b.all("dve_step"))
    dve.scalar_tensor_tensor(x, x, gain, r, ALU.mult, ALU.mult).then_inc(b.tick("normed"), 1)


def turn_for_rope(b, pe, n, turn, x):
    rows = turn.shape[0]
    pe.wait_ge(b.sem("normed"), b.nth("normed", n + 1))
    if n >= 2:
        pe.wait_ge(b.sem("turned_taken"), b.nth("turned_taken", n - 1))
    pe.matmul(b.psum[0:rows, 6 + n % 2, 0:NLAT], turn, x, start=True, stop=True).then_inc(b.tick("half_turned"), 1)


def mix_for_rope(b, dve, n, x, tmp, cos, sin):
    rows = x.shape[0]
    t = tmp[0:rows, n % 2, :]
    dve.wait_ge(b.sem("half_turned"), b.nth("half_turned", n + 1))
    dve.tensor_tensor(t, b.psum[0:rows, 6 + n % 2, 0:NLAT], sin, ALU.mult).then_inc(b.tick("turned_taken"), 1)
    dve.tensor_tensor(x, x, cos, ALU.mult).then_inc(b.tick("dve_step"), 1)
    dve.wait_ge(b.sem("dve_step"), b.all("dve_step"))
    dve.wait_ge(b.sem("turned_taken"), b.nth("turned_taken", n + 1))
    dve.tensor_tensor(x, x, t, ALU.add).then_inc(b.tick("dve_step"), 1)


def project_heads(b, l, kind, seg, m):
    d = b.dram
    rope = kind == "diff"
    gains = (C_NAQ, C_NAK) if kind == "na" else (C_DFQ, C_DFK)
    st = ExitStack()
    with st:
        sq = b.sb(st, "head_sq", [P, 2, T])
        rstd = b.sb(st, "head_rstd", [P, 2, T])
        if rope:
            tab = b.sb(st, "rope_tab", [P, 2, NLAT])
            turn = b.sb(st, "rope_turn", [P, P])
            tmp = b.sb(st, "rope_tmp", [P, 2, NLAT])
            prod = b.sb(st, "lam_prod", [64, 2])
        cols = [seg] * 4 + [ALL] * 4

        def tile(n):
            return (m["q"] if n < 4 else m["k"])[:, n % 4, cols[n][0]:cols[n][1]]

        def latents(n):
            return (m["q"] if n < 4 else m["k"])[:, n % 4, NCTX:T]

        with b.stage() as block:
            q0, _, qt, _ = b.phases[f"{kind}_qk{l}"]
            v0, _, vt, _ = b.phases[f"{kind}_v{l}"]
            z0, _, zt, _ = b.phases[f"{kind}_z{l}"]

            @block.sync
            def _(sp):
                if rope:
                    sp.dma_start(tab[:], d["c_rope_diff"]).then_inc(b.tick("rope_in", 16), 16)
                    sp.dma_start(turn[:], d["c_turn_diff"]).then_inc(b.tick("rope_in", 16), 16)
                for x in ("qk", "v", "z"):
                    b.stream(sp, f"{kind}_{x}{l}")

            @block.gpsimd
            def _(pool):
                for n in range(8):
                    b.split_weights(pool, "pool", q0 + n + AHEAD)
                    square_for_norm(b, pool, n, qt + n, tile(n), sq, P, cols[n])
                b.split_weights(pool, "pool", z0 + 3 + AHEAD)

            @block.tensor
            def _(pe):
                for n in range(8):
                    b.products(pe, f"{kind}_qk{l}", n, cols[n], b.input(cols[n]))
                    if n >= 2:
                        sum_for_norm(b, pe, n - 2, b.half_ones[:], sq, cols[n - 2])
                for s in range(VS):
                    b.products_by_token(pe, f"{kind}_v{l}", s, b.tokens)
                    if s < 2:
                        sum_for_norm(b, pe, 6 + s, b.half_ones[:], sq, cols[6 + s])
                for j in range(4):
                    b.products(pe, f"{kind}_z{l}", j, seg, b.input(seg))
                    if rope:
                        if j == 0:
                            pe.wait_ge(b.sem("rope_in"), b.nth("rope_in", 32))
                            pe.wait_ge(b.sem("lam_products"), b.nth("lam_products", 1))
                            pe.wait_ge(b.sem("deviation_ready"), b.nth("deviation_ready", 8))
                            pe.matmul(b.psum[:, 4, 0:2], b.ones[0:64, :], prod[:], start=True, stop=True)\
                                .then_inc(b.tick("lam_sums"), 1)
                        for n in (2 * j, 2 * j + 1):
                            turn_for_rope(b, pe, n, turn[:], latents(n))

            @block.scalar
            def _(act):
                b.round_weights(act, q0 + 1)
                for n in range(8):
                    b.round_weights(act, b.last_slot(qt + n) + AHEAD)
                    act.wait_ge(b.sem("product_done"), qt + n + 1)
                    act.activation(tile(n), b.bank(qt + n)[:, cols[n][0]:cols[n][1]], ACT.Copy)\
                        .then_inc(b.reads_out(qt + n), 1)
                    if n >= 3:
                        deviation_for_norm(b, act, n - 3, rstd, P, cols[n - 3], 64)
                b.round_weights(act, v0 + VS - 1)
                for n in range(5, 8):
                    deviation_for_norm(b, act, n, rstd, P, cols[n], 64)
                b.round_weights(act, v0 + VS - 1 + AHEAD)
                for j in range(TT):
                    act.wait_ge(b.sem("product_done"), vt + j + 1)
                    act.activation(m["v"][:, j, :], b.bank(vt + j), ACT.Copy).then_inc(b.reads_out(vt + j), 1)
                for j in range(4):
                    b.round_weights(act, b.last_slot(zt + j) + AHEAD)
                    act.wait_ge(b.sem("product_done"), zt + j + 1)
                    act.activation(m["z"][:, j, seg[0]:seg[1]], b.bank(zt + j)[:, seg[0]:seg[1]], ACT.Silu)\
                        .then_inc(b.reads_out(zt + j), 1)
                if rope:
                    act.wait_ge(b.sem("lam_sums"), b.nth("lam_sums", 1))
                    act.activation(b.lam[:, l, 0:2], b.psum[:, 4, 0:2], ACT.Exp).then_inc(b.tick("lam_exps"), 1)

            @block.vector
            def _(dve):
                if rope:
                    c = b.cols[0:64, C_LAM[0], C_LAM[1]:C_LAM[1] + 8].rearrange("p (a b l) -> p a b l", a=2, b=2)
                    dve.tensor_tensor(prod[:], c[:, :, 0, l], c[:, :, 1, l], ALU.mult)\
                        .then_inc(b.tick("lam_products"), 1)
                for n in range(8):
                    scale_for_norm(b, dve, n, tile(n), rstd, P, cols[n], column(b, gains[n // 4], l))
                if rope:
                    dve.wait_ge(b.sem("rope_in"), b.nth("rope_in", 32))
                    for n in range(8):
                        mix_for_rope(b, dve, n, latents(n), tmp, tab[:, 0, :], tab[:, 1, :])
                    lam0 = 0.8 - 0.6 * math.exp(-0.3 * l)
                    dve.wait_ge(b.sem("lam_exps"), b.nth("lam_exps", 1))
                    x = b.lam[:, l]
                    dve.tensor_tensor(x[:, 2:3], x[:, 1:2], x[:, 0:1], ALU.subtract).then_inc(b.tick("dve_step"), 1)
                    dve.tensor_scalar(x[:, 3:4], column(b, C_SUBLN, l), 1.0 - lam0, None, ALU.mult)\
                        .then_inc(b.tick("dve_step"), 1)
                    dve.wait_ge(b.sem("dve_step"), b.all("dve_step"))
                    dve.tensor_scalar(x[:, 2:3], x[:, 2:3], -lam0, None, ALU.add).then_inc(b.tick("dve_step"), 1)


def project_latent(b, l, seg, m):
    d = b.dram
    s0, s1 = seg
    st = ExitStack()
    with st:
        cq = b.sb(st, "mla_cq", [P, 3, T])
        ckv = b.sb(st, "mla_ckv", [P, 2, T])
        kr = b.sb(st, "mla_kr", [MQK, T])
        sq = b.sb(st, "mla_sq", [P, 2, T])
        rstd = b.sb(st, "mla_rstd", [P, 2, T])
        tab = b.sb(st, "mla_tab", [MQK, 2, NLAT])
        turn = b.sb(st, "mla_turn", [MQK, MQK])
        tmp = b.sb(st, "mla_tmp", [MQK, 2, NLAT])
        rank = [(cq, i, seg) for i in range(3)] + [(ckv, i, ALL) for i in range(2)]
        with b.stage() as block:
            q0, _, qt, _ = b.phases[f"mla_cq{l}"]
            c0, _, ct, _ = b.phases[f"mla_ckv{l}"]
            r0, _, rt, _ = b.phases[f"mla_kr{l}"]
            z0, _, zt, _ = b.phases[f"mla_z{l}"]

            @block.sync
            def _(sp):
                for x in ("cq", "ckv", "kr", "z"):
                    b.stream(sp, f"mla_{x}{l}")

            @block.gpsimd
            def _(pool):
                for n, (x, i, (a, e)) in enumerate(rank):
                    b.split_weights(pool, "pool", q0 + n + AHEAD)
                    pool.wait_ge(*b.evacuated(qt + n))
                    if n >= 2:
                        pool.wait_ge(b.sem("square_added"), b.nth("square_added", n - 1))
                    pool.tensor_tensor(sq[:, n % 2, a:e], x[:, i, a:e], x[:, i, a:e], ALU.mult)\
                        .then_inc(b.tick("squared"), 1)
                b.split_weights(pool, "pool", z0 + 3 + AHEAD)

            @block.tensor
            def _(pe):
                def sums(n):
                    x, i, (a, e) = rank[n]
                    pe.wait_ge(b.sem("squared"), b.nth("squared", n + 1))
                    pe.matmul(b.psum[:, 4 + n // 3, a:e], b.ones[:], sq[:, n % 2, a:e], start=i == 0, stop=n in (2, 4))\
                        .then_inc(b.tick("square_added"), 1)

                for j in range(3):
                    b.products(pe, f"mla_cq{l}", j, seg, b.input(seg))
                sums(0)
                for j in range(2):
                    b.products(pe, f"mla_ckv{l}", j, ALL, b.input(ALL))
                    sums(1 + j)
                b.products(pe, f"mla_kr{l}", 0, ALL, b.input(ALL))
                sums(3)
                for j in range(4):
                    b.products(pe, f"mla_z{l}", j, seg, b.input(seg))
                    if j == 0:
                        sums(4)

            @block.scalar
            def _(act):
                for n, (x, i, (a, e)) in enumerate(rank):
                    b.round_weights(act, b.last_slot(qt + n) + AHEAD)
                    act.wait_ge(b.sem("product_done"), qt + n + 1)
                    act.activation(x[:, i, a:e], b.bank(qt + n)[:, a:e], ACT.Copy).then_inc(b.reads_out(qt + n), 1)
                b.round_weights(act, r0 + AHEAD)
                act.wait_ge(b.sem("product_done"), rt + 1)
                act.activation(kr[MNOPE:MQK, :], b.bank(rt)[P - MROPE:P, :], ACT.Copy).then_inc(b.reads_out(rt), 1)
                for j in range(4):
                    b.round_weights(act, b.last_slot(zt + j) + AHEAD)
                    act.wait_ge(b.sem("product_done"), zt + j + 1)
                    act.activation(m["z"][:, j, s0:s1], b.bank(zt + j)[:, s0:s1], ACT.Silu)\
                        .then_inc(b.reads_out(zt + j), 1)
                for i, (n, (a, e), width) in enumerate(((3, seg, QL), (5, ALL, KVL))):
                    act.wait_ge(b.sem("square_added"), b.nth("square_added", n))
                    act.activation(rstd[:, i, a:e], b.psum[:, 4 + i, a:e], ACT.Sqrt, bias=b.eps[:, 1:2],
                                         scale=1.0 / width).then_inc(b.tick("deviation_ready"), 1)

            @block.vector
            def _(dve):
                for i, (a, e) in enumerate((seg, ALL)):
                    dve.wait_ge(b.sem("deviation_ready"), b.nth("deviation_ready", i + 1))
                    dve.reciprocal(rstd[:, i, a:e], rstd[:, i, a:e]).then_inc(b.tick("dve_step"), 1)
                dve.wait_ge(b.sem("dve_step"), b.all("dve_step"))
                dve.wait_ge(b.sem("squared"), b.nth("squared", 5))
                for n, (x, i, (a, e)) in enumerate(rank):
                    gain = column(b, C_CQG, 3 * l + i) if n < 3 else column(b, C_CKVG, 2 * l + i)
                    dve.scalar_tensor_tensor(x[:, i, a:e], x[:, i, a:e], gain, rstd[:, n // 3, a:e], ALU.mult, ALU.mult)

        cols = [seg] * MLH + [ALL] * MLH

        def tile(n):
            return (m["q"] if n < MLH else m["k"])[0:MQK, n % MLH, cols[n][0]:cols[n][1]]

        def latents(n):
            return (m["q"] if n < MLH else m["k"])[0:MQK, n % MLH, NCTX:T]

        with b.stage() as block:
            u0, _, ut, _ = b.phases[f"mla_uq{l}"]
            k0, _, kt, _ = b.phases[f"mla_ukv{l}"]

            @block.sync
            def _(sp):
                sp.dma_start(tab[:], d["c_rope_mla"]).then_inc(b.tick("rope_in", 16), 16)
                sp.dma_start(turn[:], d["c_turn_mla"]).then_inc(b.tick("rope_in", 16), 16)
                for x in ("uq", "ukv"):
                    b.stream(sp, f"mla_{x}{l}")

            @block.gpsimd
            def _(pool):
                for h in range(MLH):
                    pool.tensor_copy(m["k"][MNOPE:MQK, h, :], kr[MNOPE:MQK, :]).then_inc(b.tick("tails_ready"), 1)
                pool.wait_ge(b.sem("tails_ready"), b.nth("tails_ready", MLH))
                for n in range(2 * MLH):
                    square_for_norm(b, pool, n, ut + n, tile(n), sq, MQK, cols[n])
                b.split_weights(pool, "pool", k0 + 1 + AHEAD)

            @block.tensor
            def _(pe):
                for h in range(MLH):
                    n = u0 + h // UQH
                    pe.wait_ge(*b.weights_in(n))
                    b.product(pe, ut + h, lambda x: x[0:MQK, s0:s1],
                              [(b.slot(n)[:, k, h % UQH * MQK:(h % UQH + 1) * MQK], cq[:, k, s0:s1]) for k in range(3)])
                half = MLH // 2
                for h in range(MLH):
                    n = k0 + h // half
                    pe.wait_ge(*b.weights_in(n))
                    b.product(pe, kt + h, lambda x: x[0:MNOPE, :],
                              [(b.slot(n)[:, k, h % half * P:h % half * P + MNOPE], ckv[:, k, :]) for k in range(2)])
                    sum_for_norm(b, pe, h, b.ones[0:MQK, 0:MQK], sq, cols[h])
                for j in range(TT):
                    g = kt + MLH + j
                    pe.wait_ge(*b.evacuated(g - NBANK))
                    for i in range(2):
                        w = b.slot(k0 + i).rearrange("p k (h c) -> p k h c", c=P)
                        for k in range(2):
                            ins = pe.matmul(b.bank(g)[:, i * 256:(i + 1) * 256], ckv[:, k, j * P:(j + 1) * P],
                                            w[:, k, :, MNOPE:P], start=i == 0 and k == 0, stop=i == 1 and k == 1,
                                            skip_group_check=True)
                        if i == 0 and j == TT - 1:
                            ins.then_inc(b.tick("weights_used"), 1)
                    ins.then_inc(b.tick("product_done"), 1)
                pe.wait_ge(b.sem("rope_in"), b.nth("rope_in", 32))
                for n in range(MLH):
                    sum_for_norm(b, pe, MLH + n, b.ones[0:MQK, 0:MQK], sq, cols[MLH + n])
                    turn_for_rope(b, pe, n, turn[:], latents(n))
                for n in range(MLH, 2 * MLH):
                    turn_for_rope(b, pe, n, turn[:], latents(n))

            @block.scalar
            def _(act):
                for h in range(MLH):
                    act.wait_ge(b.sem("product_done"), ut + h + 1)
                    act.activation(tile(h), b.bank(ut + h)[0:MQK, s0:s1], ACT.Copy).then_inc(b.reads_out(ut + h), 1)
                for h in range(MLH):
                    act.wait_ge(b.sem("product_done"), kt + h + 1)
                    act.activation(m["k"][0:MNOPE, h, :], b.bank(kt + h)[0:MNOPE, :], ACT.Copy)\
                        .then_inc(b.reads_out(kt + h), 1)
                    deviation_for_norm(b, act, h, rstd, MQK, cols[h], MQK)
                for j in range(TT):
                    act.wait_ge(b.sem("product_done"), kt + MLH + j + 1)
                    act.activation(m["v"][:, j, :], b.bank(kt + MLH + j), ACT.Copy)\
                        .then_inc(b.reads_out(kt + MLH + j), 1)
                for n in range(MLH, 2 * MLH):
                    deviation_for_norm(b, act, n, rstd, MQK, cols[n], MQK)
                b.round_weights(act, k0 + 1 + AHEAD)

            @block.vector
            def _(dve):
                dve.wait_ge(b.sem("rope_in"), b.nth("rope_in", 32))

                def norm(n):
                    scale_for_norm(b, dve, n, tile(n), rstd, MQK, cols[n],
                                  column(b, C_MLQ if n < MLH else C_MLK, l, MQK))

                def rope(n):
                    mix_for_rope(b, dve, n, latents(n), tmp, tab[:, 0, :], tab[:, 1, :])

                for n in range(MLH):
                    norm(n)
                for n in range(MLH):
                    norm(MLH + n)
                    rope(n)
                for n in range(MLH, 2 * MLH):
                    rope(n)


def attend(b, l, r, m, last):
    d = b.dram
    near, diffs = r == 0, r == 2
    scale = (64 if r != 1 else MQK) ** -0.5
    VW = P if diffs else 64
    MAPS = 8
    groups = [(seg, t) for seg in ((LAT,) if last else (LAT, CTX)) for t in range(2)]
    units = [(gq, u) for gq in range(len(groups)) for u in range(MAPS)]
    N = len(units)
    NEAR = 2 * MAPS if near else 0
    st = ExitStack()
    with st:
        prob = b.sb(st, "prob", [P, 2, T])
        probT = b.sb(st, "probT", [P, 2, T])
        top = b.sb(st, "row_top", [P, 2, 2])
        den = b.sb(st, "row_sum", [P, len(groups), MAPS])
        rows = b.sb(st, "out_rows", [P, MAPS * VW])
        if near:
            biased = b.sb(st, "biased", [P, 2, T])
            bias = b.sb(st, "bias_tile", [P, 2, T])
            mask = b.sb(st, "na_mask", [P, NLAT])
        if diffs:
            sub = b.sb(st, "diff_rows", [P, DFH, P])
            ss = b.sb(st, "diff_ss", [P, len(groups), DFH])
            sq = b.sb(st, "diff_sq", [P, DFH, P])

        def keys(n):
            return T if groups[units[n][0]][0] == LAT else NCTX

        def head_rows(u):
            return slice(0, MQK) if r == 1 else slice(64 * (u % 2), 64 * (u % 2) + 64)

        def qcols(gq):
            seg, t = groups[gq]
            return slice(seg[0] + t * P, seg[0] + (t + 1) * P)

        def out_bank(gq, u):
            return (u // 4, u % 4 * P) if diffs else (gq % 2, u * 64)

        with b.stage() as block:

            @block.sync
            def _(sp):
                if near:
                    sp.dma_start(mask[:], d["c_na_mask"]).then_inc(b.tick("mask_in", 16), 16)
                    for n in range(NEAR):
                        gq, u = units[n]
                        if n >= 2:
                            sp.wait_ge(b.sem("scores_biased"), b.nth("scores_biased", n - 1))
                        sp.dma_start(bias[:, n % 2, NCTX:T], d["na_bias"][l, u, gq * P:(gq + 1) * P, :])\
                            .then_inc(b.tick(f"bias_in_{n % 2}", 16), 16)

            @block.gpsimd
            def _(pool):
                if near:
                    pool.memset(bias[:, :, 0:NCTX], 0.0).then_inc(b.tick("bias_cleared"), 1)
                    pool.wait_ge(b.sem("bias_cleared"), b.nth("bias_cleared", 1))
                    pool.wait_ge(b.sem("mask_in"), b.nth("mask_in", 16))
                    for n in range(NEAR):
                        pool.wait_ge(b.sem(f"bias_in_{n % 2}"), b.nth(f"bias_in_{n % 2}", 16 * (n // 2 + 1)))
                        x = bias[:, n % 2, NCTX:T]
                        pool.tensor_tensor(x, x, mask[:], ALU.add).then_inc(b.tick("bias_ready"), 1)

            @block.tensor
            def _(pe):
                def scores(n):
                    gq, u = units[n]
                    if n >= 2:
                        pe.wait_ge(b.sem("prob_ready"), b.nth("prob_ready", n - 1))
                    t = u if r == 1 else u // 2
                    pe.matmul(b.psum[:, 4 + n % 2, 0:keys(n)], m["q"][head_rows(u), t, qcols(gq)],
                                    m["k"][head_rows(u), t, 0:keys(n)], start=True, stop=True)\
                                        .then_inc(b.tick("scores_ready"), 1)

                def turn(n):
                    pe.wait_ge(b.sem("prob_ready"), b.nth("prob_ready", n + 1))
                    if n >= 2:
                        pe.wait_ge(b.sem("turned_copied"), b.nth("turned_copied", n - 1))
                    for t in range(keys(n) // P):
                        ins = pe.transpose(b.psum[:, 6 + n % 2, t * P:(t + 1) * P], prob[:, n % 2, t * P:(t + 1) * P],
                                           b.ident[:])
                    ins.then_inc(b.tick("prob_turned"), 1)

                def values(n):
                    gq, u = units[n]
                    pe.wait_ge(b.sem("turned_copied"), b.nth("turned_copied", n + 1))
                    if u == 0 and gq >= (1 if diffs else 2):
                        pe.wait_ge(b.sem("rows_ready"), b.nth("rows_ready", gq if diffs else gq - 1))
                    bank, c = out_bank(gq, u)
                    h = u // 2 if diffs else u
                    nt = keys(n) // P
                    for t in range(nt):
                        ins = pe.matmul(b.psum[:, bank, c:c + VW], probT[:, n % 2, t * P:(t + 1) * P],
                                        m["v"][:, t, h * VW:(h + 1) * VW], start=c == 0 and t == 0,
                                        stop=t == nt - 1 and c + VW == 512, skip_group_check=True)
                    ins.then_inc(b.tick("values_mixed"), 1)
                def turn_rows(gq):
                    pe.wait_ge(b.sem("rows_final" if diffs else "rows_ready"), b.nth("rows_final" if diffs else "rows_ready", gq + 1))
                    if gq >= 2:
                        pe.wait_ge(b.sem("gated"), b.nth("gated", gq - 1))
                    src = sub[:].rearrange("p h v -> p (h v)") if diffs else rows[:]
                    for t in range(4):
                        ins = pe.transpose(b.psum[:, 2 + gq % 2, t * P:(t + 1) * P], src[:, t * P:(t + 1) * P], b.ident[:])
                    ins.then_inc(b.tick("rows_turned"), 1)

                scores(0)
                for n in range(N):
                    if n + 1 < N:
                        scores(n + 1)
                    turn(n)
                    if n:
                        values(n - 1)
                    if units[n][0] and units[n][1] == 3:
                        turn_rows(units[n][0] - 1)
                values(N - 1)
                turn_rows(len(groups) - 1)

            @block.scalar
            def _(act):
                def copy(n):
                    act.wait_ge(b.sem("prob_turned"), b.nth("prob_turned", n + 1))
                    if n >= 2:
                        act.wait_ge(b.sem("values_mixed"), b.nth("values_mixed", n - 1))
                    k = keys(n)
                    act.activation(probT[:, n % 2, 0:k], b.psum[:, 6 + n % 2, 0:k], ACT.Copy)\
                        .then_inc(b.tick("turned_copied"), 1)

                for n in range(N):
                    gq, u = units[n]
                    act.wait_ge(b.sem("top_ready"), b.nth("top_ready", n + 1))
                    if n >= 2:
                        act.wait_ge(b.sem("prob_turned"), b.nth("prob_turned", n - 1))
                    k = keys(n)
                    src, sc = (biased[:, n % 2, :], 1.0) if n < NEAR else (b.psum[:, 4 + n % 2, 0:k], scale)
                    act.activation(prob[:, n % 2, 0:k], src, ACT.Exp, bias=top[:, n % 2, 1:2], scale=sc,
                                         accum_out=den[:, gq, u:u + 1]).then_inc(b.tick("prob_ready"), 1)
                    if n:
                        copy(n - 1)
                    if diffs and u == 1 and gq:
                        deviation(b, act, gq - 1, ss)
                copy(N - 1)
                if diffs:
                    deviation(b, act, len(groups) - 1, ss)

            @block.vector
            def _(dve):
                if near:
                    dve.wait_ge(b.sem("bias_cleared"), b.nth("bias_cleared", 1))

                def maxima(n):
                    dve.wait_ge(b.sem("scores_ready"), b.nth("scores_ready", n + 1))
                    k = keys(n)
                    src = b.psum[:, 4 + n % 2, 0:k]
                    if n >= 2:
                        dve.wait_ge(b.sem("prob_ready"), b.nth("prob_ready", n - 1))
                    if n < NEAR:
                        dve.wait_ge(b.sem("bias_ready"), b.nth("bias_ready", n + 1))
                        dve.scalar_tensor_tensor(biased[:, n % 2, :], src, scale, bias[:, n % 2, :], ALU.mult, ALU.add)\
                            .then_inc(b.tick("scores_biased"), 1)
                        dve.wait_ge(b.sem("scores_biased"), b.nth("scores_biased", n + 1))
                        src = biased[:, n % 2, :]
                    dve.reduce_max(top[:, n % 2, 0:1], src, AX_X).then_inc(b.tick("dve_step"), 1)
                    dve.wait_ge(b.sem("dve_step"), b.all("dve_step"))
                    dve.tensor_scalar(top[:, n % 2, 1:2], top[:, n % 2, 0:1], -1.0 if n < NEAR else -scale, None,
                                            ALU.mult).then_inc(b.tick("top_ready"), 1)

                def finish(gq):
                    dve.wait_ge(b.sem("values_mixed"), b.nth("values_mixed", (gq + 1) * MAPS))
                    dve.wait_ge(b.sem("prob_ready"), b.nth("prob_ready", (gq + 1) * MAPS))
                    if gq:
                        dve.wait_ge(b.sem("rows_turned"), b.nth("rows_turned", gq))
                    x = den[:, gq, :]
                    dve.reciprocal(x, x).then_inc(b.tick("dve_step"), 1)
                    dve.wait_ge(b.sem("dve_step"), b.all("dve_step"))
                    if diffs:
                        y = x.rearrange("p (h a) -> p h a", a=2)[:, :, 1]
                        dve.tensor_scalar(y, y, b.lam[:, l, 2:3], None, ALU.mult).then_inc(b.tick("dve_step"), 1)
                        dve.wait_ge(b.sem("dve_step"), b.all("dve_step"))
                    width = MAPS * VW
                    o = b.psum[:, 0:2, :].rearrange("p b n -> p (b n)") if diffs else b.psum[:, gq % 2, :]
                    dve.tensor_tensor(rows[:].rearrange("p (u v) -> p u v", v=VW), o.rearrange("p (u v) -> p u v", v=VW),
                                            x.unsqueeze(2).broadcast_to([P, MAPS, VW]), ALU.mult)\
                                                .then_inc(b.tick("rows_ready"), 1)
                    if diffs:
                        dve.wait_ge(b.sem("rows_ready"), b.nth("rows_ready", gq + 1))
                        y = rows[:].rearrange("p (h a v) -> p h a v", a=2, v=VW)
                        dve.tensor_tensor(sub[:], y[:, :, 0, :], y[:, :, 1, :], ALU.add)\
                            .then_inc(b.tick("dve_step"), 1)
                        dve.wait_ge(b.sem("dve_step"), b.all("dve_step"))
                        dve.tensor_tensor(sq[:], sub[:], sub[:], ALU.mult).then_inc(b.tick("dve_step"), 1)
                        dve.wait_ge(b.sem("dve_step"), b.all("dve_step"))
                        dve.reduce_sum(ss[:, gq, :], sq[:], AX_X).then_inc(b.tick("squares_summed"), 1)

                def subnorm(gq):
                    dve.wait_ge(b.sem("deviation_ready"), b.nth("deviation_ready", gq + 1))
                    x = ss[:, gq, :]
                    dve.reciprocal(x, x).then_inc(b.tick("dve_step"), 1)
                    dve.wait_ge(b.sem("dve_step"), b.all("dve_step"))
                    dve.tensor_tensor(sub[:], sub[:], x.unsqueeze(2).broadcast_to([P, DFH, P]), ALU.mult)\
                        .then_inc(b.tick("rows_final"), 1)

                def gate(gq):
                    dve.wait_ge(b.sem("rows_turned"), b.nth("rows_turned", gq + 1))
                    o = b.psum[:, 2 + gq % 2, :].rearrange("p (t q) -> p t q", q=P)
                    dst, z = m["o"][:, r, :, qcols(gq)], m["z"][:, :, qcols(gq)]
                    if diffs:
                        ins = dve.scalar_tensor_tensor(dst, o, b.lam[:, l, 3:4], z, ALU.mult, ALU.mult)
                    else:
                        ins = dve.tensor_tensor(dst, o, z, ALU.mult)
                    ins.then_inc(b.tick("gated"), 1)

                for n in range(N):
                    gq, u = units[n]
                    maxima(n)
                    if gq and u == 1:
                        finish(gq - 1)
                    if gq and u == 2 and diffs:
                        subnorm(gq - 1)
                    if gq and u == 4:
                        gate(gq - 1)
                finish(len(groups) - 1)
                if diffs:
                    subnorm(len(groups) - 1)
                gate(len(groups) - 1)


def deviation(b, act, gq, ss):
    act.wait_ge(b.sem("squares_summed"), b.nth("squares_summed", gq + 1))
    x = ss[:, gq, :]
    act.activation(x, x, ACT.Sqrt, bias=b.eps[:, 1:2], scale=1.0 / P).then_inc(b.tick("deviation_ready"), 1)


def merge(b, l, seg, o):
    a, e = seg
    n = e - a
    st = ExitStack()
    with st:
        tmp = b.sb(st, "merge_tmp", [P, 2, T])
        sig = b.sb(st, "merge_gate", [P, KD, T])
        y = b.sb(st, "merge_sum", [P, KD, T])
        oh = b.sb(st, "merge_o_hi", [P, BW // P, T])
        ol = b.sb(st, "merge_o_lo", [P, BW // P, T])
        oh_r, ol_r = oh[:].bitcast(F32R), ol[:].bitcast(F32R)
        with b.stage() as block:
            gates = [b.phases[f"gate{l}_{r}"] for r in range(3)]
            brs = [b.phases[f"branch{l}_{r}"] for r in range(3)]
            w0, _, wt, _ = b.phases[f"merge{l}"]

            @block.sync
            def _(sp):
                for r in range(3):
                    b.stream(sp, f"gate{l}_{r}")
                    b.stream(sp, f"branch{l}_{r}")
                b.stream(sp, f"merge{l}")

            @block.tensor
            def _(pe):
                for r in range(3):
                    for j in range(KD):
                        b.products(pe, f"gate{l}_{r}", j, seg, b.input(seg))
                    s0, _, t0, _ = brs[r]
                    pe.wait_ge(b.sem("branch_split"), b.nth("branch_split", r + 1))
                    for j in range(KD):
                        pe.wait_ge(*b.weights_split(s0 + j // 2))
                        b.product(pe, t0 + j, lambda x: x[:, a:e],
                                  b.passes(s0 + j // 2, slice(j % 2 * P, (j % 2 + 1) * P),
                                           lambda k: (oh_r[:, k, a:e], ol_r[:, k, a:e])))
                pe.wait_ge(b.sem("sum_split"), b.nth("sum_split", KD))
                for j in range(KD):
                    b.products(pe, f"merge{l}", j, seg, b.input(seg))

            @block.scalar
            def _(act):
                for r in range(3):
                    for j in range(KD):
                        g = gates[r][2] + j
                        b.round_weights(act, b.last_slot(g) + AHEAD)
                        if j == 2:
                            if r:
                                act.wait_ge(*b.evacuated(brs[r - 1][2] + KD - 1))
                            act.activation(oh_r[:, :, a:e], o[:, r, :, a:e], ACT.Copy)\
                                .then_inc(b.tick("branch_rounded"), 1)
                        act.wait_ge(b.sem("product_done"), g + 1)
                        if r:
                            act.wait_ge(*b.evacuated(brs[r - 1][2] + j))
                        act.activation(sig[:, j, a:e], b.bank(g)[:, a:e], ACT.Sigmoid).then_inc(b.reads_out(g), 1)
                b.round_weights(act, w0 + 1)
                for j in range(KD):
                    act.wait_ge(b.sem("branch_added"), b.nth("branch_added", KD + j + 1))
                    act.activation(b.UH_r[:, j, a:e], y[:, j, a:e], ACT.Copy).then_inc(b.tick("sum_rounded"), 1)
                b.round_weights(act, w0 + KD - 1 + AHEAD)

            @block.gpsimd
            def _(pool):
                for r in (1, 2):
                    for j in range(KD):
                        i = (r - 1) * KD + j
                        pool.wait_ge(*b.evacuated(brs[r][2] + j))
                        if r == 2:
                            pool.wait_ge(b.sem("branch_added"), b.nth("branch_added", j + 1))
                        pool.tensor_tensor(y[:, j, a:e], y[:, j, a:e], tmp[:, i % 2, a:e], ALU.add)\
                            .then_inc(b.tick("branch_added"), 1)

            @block.vector
            def _(dve):
                b.split_weights(dve, "dve", gates[0][0] + 1)
                for r in range(3):
                    b.split_weights(dve, "dve", gates[r][0] + KD - 2)
                    dve.wait_ge(b.sem("branch_rounded"), b.nth("branch_rounded", r + 1))
                    dve.tensor_tensor(ol_r[:, :, a:e], o[:, r, :, a:e], oh[:, :, a:e], ALU.subtract)\
                        .then_inc(b.tick("branch_split"), 1)
                    b.split_weights(dve, "dve", gates[r][0] + KD - 1)
                    for j in range(KD):
                        g = brs[r][2] + j
                        b.split_weights(dve, "dve", b.last_slot(g) + 1)
                        dve.wait_ge(b.sem("product_done"), g + 1)
                        dve.wait_ge(*b.evacuated(gates[r][2] + j))
                        i = (r - 1) * KD + j
                        if i >= 2:
                            dve.wait_ge(b.sem("branch_added"), b.nth("branch_added", i - 1))
                        dst = y[:, j, a:e] if r == 0 else tmp[:, i % 2, a:e]
                        dve.tensor_tensor(dst, b.bank(g)[:, a:e], sig[:, j, a:e], ALU.mult)\
                            .then_inc(b.reads_out(g), 1)
                b.split_weights(dve, "dve", w0 + 1)
                for j in range(KD):
                    dve.wait_ge(b.sem("sum_rounded"), b.nth("sum_rounded", j + 1))
                    dve.tensor_tensor(b.UL_r[:, j, a:e], y[:, j, a:e], b.UH[:, j, a:e], ALU.subtract)\
                        .then_inc(b.tick("sum_split"), 1)
                for j in range(KD):
                    b.split_weights(dve, "dve", b.last_slot(wt + j) + AHEAD)
                    dve.wait_ge(b.sem("product_done"), wt + j + 1)
                    for v, (s, t) in enumerate((LAT, CTX)):
                        if seg == LAT and v == 1:
                            continue
                        ins = dve.scalar_tensor_tensor(b.H2[:, j, s:t], b.bank(wt + j)[:, s:t],
                                                       b.mod2[:, l, 2 * KD + j, v:v + 1], b.H2[:, j, s:t], ALU.mult, ALU.add)
                    ins.then_inc(b.reads_out(wt + j), 1)


def store_stage(b, src, out, dump):
    st = ExitStack()
    with st:
        tok = b.sb(st, "out_tokens", [P, 2, D])
        with b.stage() as block:

            @block.tensor
            def _(pe):
                for n in range(2 * KD):
                    t, k = n // KD, n % KD
                    if n >= 4:
                        pe.wait_ge(b.sem("tile_copied"), b.nth("tile_copied", n - 3))
                    pe.matmul(b.psum[:, 4 + n % 4, 0:P], src[:, k, NCTX + t * P:NCTX + (t + 1) * P], b.ident[:],
                                    start=True, stop=True).then_inc(b.tick("tile_turned"), 1)
                for n in range(4):
                    pe.wait_ge(b.sem("tile_copied"), b.nth("tile_copied", 2 * KD))
                    t, c = n // 2, n % 2
                    pe.matmul(b.psum[:, n, :], b.snake[:], tok[:, t, c * 512:(c + 1) * 512], start=True,
                                    stop=True).then_inc(b.tick("row_ordered"), 1)

            @block.vector
            def _(dve):
                for n in range(2 * KD):
                    t, k = n // KD, n % KD
                    dve.wait_ge(b.sem("tile_turned"), b.nth("tile_turned", n + 1))
                    dve.tensor_copy(tok[:, t, k * P:(k + 1) * P], b.psum[:, 4 + n % 4, 0:P])\
                        .then_inc(b.tick("tile_copied"), 1)
                for n in range(4):
                    t, c = n // 2, n % 2
                    dve.wait_ge(b.sem("row_ordered"), b.nth("row_ordered", 4))
                    dve.tensor_copy(tok[:, t, c * 512:(c + 1) * 512], b.psum[:, n, :])\
                        .then_inc(b.tick("output_ready"), 1)

            @block.sync
            def _(sp):
                sp.wait_ge(b.sem("output_ready"), b.nth("output_ready", 4))
                sp.dma_start(out[0].rearrange("(t p) n -> p t n", p=P), tok[:]).then_inc(b.tick("stored", 16), 16)
                for name, ap in (dump(b) if dump else {}).items():
                    sp.dma_start(b.dram[name], ap).then_inc(b.tick("stored", 16), 16)
                sp.wait_ge(b.sem("stored"), b.all("stored"))


def constants():
    import numpy as np

    f = np.float32
    i = np.arange(P)
    same = i[:, None] // ROW == i[None, :] // ROW
    snake = np.where(i < ROW, i, P + ROW - 1 - i)
    c = {
        "c_ident": np.eye(P, dtype=f),
        "c_snake": np.eye(P, dtype=f)[snake],
        "c_ones": np.ones((P, P), f),
        "c_half_ones": same.astype(f),
        "c_reset": np.broadcast_to((np.arange(T) % ROW != 0).astype(f), (P, T)).copy(),
        "c_diag2": 2 * np.eye(P, dtype=f),
    }
    masks = []
    for z in range(2):
        for s in LEVELS:
            blk = i // s
            early, late = blk % 2 == 0, blk % 2 == 1
            pair = (i[:, None] // (2 * s) == i[None, :] // (2 * s)) & same
            key, query = (early, late) if z == 0 else (late, early)
            masks.append(pair & key[:, None] & query[None, :])
    c["c_causal"] = np.stack([same & (i[:, None] <= i[None, :]), same & (i[:, None] >= i[None, :])], 1).astype(f)
    row, pos = snake_tokens()
    start = np.clip(pos - 8, 0, ROW - 16)
    near = (pos[None, :] >= start[:, None]) & (pos[None, :] < start[:, None] + 16)
    c["c_na_mask"] = np.where(near, 0, -1e30).astype(f)[0:P]
    for name, rot, at, width in (("mla", MROPE, MNOPE, MQK), ("diff", 64, 0, P)):
        nf = rot // 4
        inv = f(10000.0) ** (-np.arange(nf, dtype=f) / f(nf))
        ang = np.concatenate([row.astype(f)[:, None] * inv, pos.astype(f)[:, None] * inv], 1).T
        tab = np.stack([np.ones((width, NLAT), f), np.zeros((width, NLAT), f)], 1)
        turn = np.zeros((width, width), f)
        for o in range(at, width, rot):
            for h in range(2):
                tab[o + h * rot // 2:o + (h + 1) * rot // 2, 0] = np.cos(ang)
                tab[o + h * rot // 2:o + (h + 1) * rot // 2, 1] = np.sin(ang)
            for j in range(rot // 2):
                turn[o + j + rot // 2, o + j] = -1
                turn[o + j, o + j + rot // 2] = 1
        c[f"c_rope_{name}"], c[f"c_turn_{name}"] = tab, turn
    c["c_gla_masks"] = np.stack(masks, 1).reshape(P, -1).astype(f)
    return c


def snake_tokens():
    import numpy as np

    t = np.arange(NLAT)
    row, c = t // ROW, t % ROW
    return row, np.where(row % 2 == 0, c, ROW - 1 - c)


def layouts(inputs):
    import numpy as np

    row, c = snake_tokens()
    dr = row[None, :] - row[:, None] + 7
    dc = np.clip(c[None, :] - c[:, None], -15, 15) + 15
    return {"na_bias": np.ascontiguousarray(np.asarray(inputs["na_rpb_2"])[:, :, dr, dc])}


_SKIP = ("hy_",)


def kernel(**inputs):
    import numpy as np
    import concourse.bacc as bacc
    from concourse.bass_utils import run_bass_kernel_spmd as run

    nc = bacc.Bacc("TRN2", target_bir_lowering=False, num_devices=1)
    arrays = {n: np.ascontiguousarray(a) for n, a in inputs.items() if not n.startswith(_SKIP)}
    arrays.update(layouts(arrays))
    arrays.update(constants())
    dram = {n: nc.dram_tensor(n, a.shape, mybir.dt.from_np(a.dtype), kind="ExternalInput").ap()
            for n, a in arrays.items()}
    out = nc.dram_tensor("out", (1, NLAT, D), F32, kind="ExternalOutput").ap()
    build(nc, dram, out)
    return run(nc, [arrays], core_ids=[0]).results[0]["out"]
```
